# Optimizing a Trainium2 kernel written in Bass

```python
import math
import jax, jax.numpy as jnp
from jax import lax
import numpy as np

D_MODEL = 1024
BATCH = 1
SEQ = 256
DEPTH = 2

N_A_LAYERS = DEPTH // 2
N_B_LAYERS = DEPTH - N_A_LAYERS
A_HEADS = 16
A_HEAD_DIM = D_MODEL // A_HEADS
MOBA_BLOCK = 256
MOBA_TOPK = 3
MOBA_QCHUNK = 64
B_HEADS = 8
B_HEAD_DIM = D_MODEL // (2 * B_HEADS)
B_QBLOCK = 128
D_FF = 128 * (-(-8 * D_MODEL // (3 * 128)))
CONV_WIDTH = 3
ROPE_THETA = 500000.0
ROPE_FRACTION = 4
LN_EPS = 1e-5
SUBLN_EPS = 1e-5
DEEPNORM_ALPHA = (2 * DEPTH) ** 0.25
DEEPNORM_BETA = (8 * DEPTH) ** -0.25

kernel_name = "yoco_moba_diffattn_convffn_deepnorm"

def partial_rotary(x, positions):
    rot = x.shape[-1] // ROPE_FRACTION
    half = rot // 2
    inv_freq = 1.0 / (ROPE_THETA ** (jnp.arange(half, dtype=jnp.float32) * 2.0 / rot))
    ang = positions.astype(jnp.float32)[:, :, None] * inv_freq
    cos = jnp.cos(ang)[:, :, None, :].astype(x.dtype)
    sin = jnp.sin(ang)[:, :, None, :].astype(x.dtype)
    x1, x2, xp = x[..., :half], x[..., half:rot], x[..., rot:]
    return jnp.concatenate([x1 * cos - x2 * sin, x2 * cos + x1 * sin, xp], axis=-1)

def layer_norm(x, g, b):
    xf = x.astype(jnp.float32)
    mu = jnp.mean(xf, axis=-1, keepdims=True)
    var = jnp.mean(jnp.square(xf - mu), axis=-1, keepdims=True)
    return ((xf - mu) * lax.rsqrt(var + LN_EPS) * g + b).astype(x.dtype)

def conv_ffn(x, w_in, conv_w, conv_b, w_out):
    up, gate = jnp.split(x @ w_in, 2, axis=-1)
    up = lax.conv_general_dilated(
        up, conv_w[:, None, :], window_strides=(1,),
        padding=[(CONV_WIDTH - 1, 0)],
        dimension_numbers=("NWC", "WIO", "NWC"),
        feature_group_count=up.shape[-1]) + conv_b
    return (jax.nn.gelu(up) * gate) @ w_out

def moba_attention(q, k, v):
    B, H, S, Dh = q.shape
    nb = -(-S // MOBA_BLOCK)
    pad = nb * MOBA_BLOCK - S
    kb = jnp.pad(k, ((0, 0), (0, 0), (0, pad), (0, 0))).reshape(B, H, nb, MOBA_BLOCK, Dh)
    vb = jnp.pad(v, ((0, 0), (0, 0), (0, pad), (0, 0))).reshape(B, H, nb, MOBA_BLOCK, Dh)
    scale = Dh ** -0.5
    k_mean = jnp.mean(kb, axis=3)
    gate = jnp.einsum("bhsd,bhnd->bhsn", q, k_mean).astype(jnp.float32)
    q_block = jnp.arange(S) // MOBA_BLOCK
    past = jnp.arange(nb)[None, :] < q_block[:, None]
    gate = jnp.where(past, gate, -jnp.inf)
    topk = min(MOBA_TOPK, nb)
    _, sel = lax.top_k(gate, topk)
    sel_valid = sel < q_block[:, None]
    gather = jax.vmap(jax.vmap(lambda blocks, idx: blocks[idx]))

    def chunk(c):
        start = c * MOBA_QCHUNK
        qc = lax.dynamic_slice_in_dim(q, start, MOBA_QCHUNK, axis=2)
        selc = lax.dynamic_slice_in_dim(sel, start, MOBA_QCHUNK, axis=2)
        validc = lax.dynamic_slice_in_dim(sel_valid, start, MOBA_QCHUNK, axis=2)
        k_sel = gather(kb, selc)
        v_sel = gather(vb, selc)
        own = start // MOBA_BLOCK
        k_own = lax.dynamic_index_in_dim(kb, own, axis=2, keepdims=False)
        v_own = lax.dynamic_index_in_dim(vb, own, axis=2, keepdims=False)
        s_sel = jnp.einsum("bhqd,bhqjld->bhqjl", qc, k_sel).astype(jnp.float32) * scale
        s_sel = jnp.where(validc[..., None], s_sel, -jnp.inf).reshape(B, H, MOBA_QCHUNK, topk * MOBA_BLOCK)
        q_pos = start + jnp.arange(MOBA_QCHUNK)
        k_pos = own * MOBA_BLOCK + jnp.arange(MOBA_BLOCK)
        s_own = jnp.einsum("bhqd,bhld->bhql", qc, k_own).astype(jnp.float32) * scale
        s_own = jnp.where(k_pos[None, :] <= q_pos[:, None], s_own, -jnp.inf)
        p = jax.nn.softmax(jnp.concatenate([s_sel, s_own], axis=-1), axis=-1)
        p_sel = p[..., :topk * MOBA_BLOCK].reshape(B, H, MOBA_QCHUNK, topk, MOBA_BLOCK).astype(v.dtype)
        p_own = p[..., topk * MOBA_BLOCK:].astype(v.dtype)
        return (jnp.einsum("bhqjl,bhqjld->bhqd", p_sel, v_sel)
                + jnp.einsum("bhql,bhld->bhqd", p_own, v_own))

    outs = lax.map(chunk, jnp.arange(S // MOBA_QCHUNK))
    return outs.transpose(1, 2, 0, 3, 4).reshape(B, H, S, Dh)

def diff_attention(q1, q2, k1, k2, v, lam):
    S = q1.shape[2]
    scale = q1.shape[-1] ** -0.5
    k_pos = jnp.arange(S)

    def block(i):
        start = i * B_QBLOCK
        q1b = lax.dynamic_slice_in_dim(q1, start, B_QBLOCK, axis=2)
        q2b = lax.dynamic_slice_in_dim(q2, start, B_QBLOCK, axis=2)
        mask = k_pos[None, :] <= (start + jnp.arange(B_QBLOCK))[:, None]

        def attn_map(qb, kk):
            s = jnp.einsum("bhqd,bhkd->bhqk", qb, kk).astype(jnp.float32) * scale
            return jax.nn.softmax(jnp.where(mask, s, -jnp.inf), axis=-1)

        a = attn_map(q1b, k1) - lam * attn_map(q2b, k2)
        return jnp.einsum("bhqk,bhkd->bhqd", a.astype(v.dtype), v)

    outs = lax.map(block, jnp.arange(S // B_QBLOCK))
    B, H, _, Dv = v.shape
    return outs.transpose(1, 2, 0, 3, 4).reshape(B, H, S, Dv)

def setup_inputs(seed: int = 0) -> dict:
    key = jax.random.key(seed)
    ks = jax.random.split(key, 16)
    D = D_MODEL
    f32 = jnp.float32
    nrm = lambda k, shape, s: jax.random.normal(k, shape, f32) * s
    x = jax.random.normal(ks[0], (BATCH, SEQ, D), f32)
    offsets = jax.random.randint(ks[1], (BATCH, 1), 0, 1024, dtype=jnp.int32)
    positions = offsets + jnp.arange(SEQ, dtype=jnp.int32)[None, :]
    qkv_scale = jnp.concatenate([jnp.ones((2 * D,), f32), jnp.full((D,), DEEPNORM_BETA, f32)])
    a_w_qkv = nrm(ks[2], (N_A_LAYERS, D, 3 * D), D ** -0.5) * qkv_scale
    a_w_o = nrm(ks[3], (N_A_LAYERS, D, D), D ** -0.5 * DEEPNORM_BETA)
    kv_scale = jnp.concatenate([jnp.ones((D,), f32), jnp.full((D,), DEEPNORM_BETA, f32)])
    w_kv_shared = nrm(ks[4], (D, 2 * D), D ** -0.5) * kv_scale
    b_w_q = nrm(ks[5], (N_B_LAYERS, D, D), D ** -0.5)
    b_w_o = nrm(ks[6], (N_B_LAYERS, D, D), D ** -0.5 * DEEPNORM_BETA)
    b_lambda = nrm(ks[7], (N_B_LAYERS, 4, B_HEAD_DIM), 0.1)
    b_subln_g = 1.0 + nrm(ks[8], (N_B_LAYERS, 2 * B_HEAD_DIM), 0.02)
    ln_g = 1.0 + nrm(ks[9], (DEPTH, 2, D), 0.02)
    ln_b = nrm(ks[10], (DEPTH, 2, D), 0.02)
    ffn_w_in = nrm(ks[11], (DEPTH, D, 2 * D_FF), D ** -0.5)
    ffn_conv_w = nrm(ks[12], (DEPTH, CONV_WIDTH, D_FF), CONV_WIDTH ** -0.5)
    ffn_conv_b = nrm(ks[13], (DEPTH, D_FF), 0.01)
    ffn_w_out = nrm(ks[14], (DEPTH, D_FF, D), D_FF ** -0.5 * DEEPNORM_BETA)
    return {"x": x, "positions": positions, "a_w_qkv": a_w_qkv, "a_w_o": a_w_o,
            "w_kv_shared": w_kv_shared, "b_w_q": b_w_q, "b_w_o": b_w_o,
            "b_lambda": b_lambda, "b_subln_g": b_subln_g, "ln_g": ln_g, "ln_b": ln_b,
            "ffn_w_in": ffn_w_in, "ffn_conv_w": ffn_conv_w, "ffn_conv_b": ffn_conv_b,
            "ffn_w_out": ffn_w_out}

def reference(x, positions, a_w_qkv, a_w_o, w_kv_shared, b_w_q, b_w_o, b_lambda,
              b_subln_g, ln_g, ln_b, ffn_w_in, ffn_conv_w, ffn_conv_b, ffn_w_out):
    B, S, D = x.shape
    k1 = k2 = v_sh = None
    for layer in range(DEPTH):
        if layer < N_A_LAYERS:
            qkv = (x @ a_w_qkv[layer]).reshape(B, S, 3, A_HEADS, A_HEAD_DIM)
            q = partial_rotary(qkv[:, :, 0], positions).transpose(0, 2, 1, 3)
            k = partial_rotary(qkv[:, :, 1], positions).transpose(0, 2, 1, 3)
            v = qkv[:, :, 2].transpose(0, 2, 1, 3)
            o = moba_attention(q, k, v).transpose(0, 2, 1, 3).reshape(B, S, D)
            x = layer_norm(DEEPNORM_ALPHA * x + o @ a_w_o[layer], ln_g[layer, 0], ln_b[layer, 0])
        else:
            j = layer - N_A_LAYERS
            if j == 0:
                kv = x @ w_kv_shared
                kk = partial_rotary(kv[..., :D].reshape(B, S, 2 * B_HEADS, B_HEAD_DIM), positions)
                kk = kk.reshape(B, S, B_HEADS, 2, B_HEAD_DIM)
                k1 = kk[:, :, :, 0].transpose(0, 2, 1, 3)
                k2 = kk[:, :, :, 1].transpose(0, 2, 1, 3)
                v_sh = kv[..., D:].reshape(B, S, B_HEADS, 2 * B_HEAD_DIM).transpose(0, 2, 1, 3)
            lambda_init = 0.8 - 0.6 * math.exp(-0.3 * layer)
            lp = b_lambda[j].astype(jnp.float32)
            lam = jnp.exp(jnp.sum(lp[0] * lp[1])) - jnp.exp(jnp.sum(lp[2] * lp[3])) + lambda_init
            qq = partial_rotary((x @ b_w_q[j]).reshape(B, S, 2 * B_HEADS, B_HEAD_DIM), positions)
            qq = qq.reshape(B, S, B_HEADS, 2, B_HEAD_DIM)
            q1 = qq[:, :, :, 0].transpose(0, 2, 1, 3)
            q2 = qq[:, :, :, 1].transpose(0, 2, 1, 3)
            o = diff_attention(q1, q2, k1, k2, v_sh, lam).astype(jnp.float32)
            o = o * lax.rsqrt(jnp.mean(jnp.square(o), axis=-1, keepdims=True) + SUBLN_EPS)
            o = (o * b_subln_g[j] * (1.0 - lambda_init)).astype(x.dtype)
            o = o.transpose(0, 2, 1, 3).reshape(B, S, D)
            x = layer_norm(DEEPNORM_ALPHA * x + o @ b_w_o[j], ln_g[layer, 0], ln_b[layer, 0])
        f = conv_ffn(x, ffn_w_in[layer], ffn_conv_w[layer], ffn_conv_b[layer], ffn_w_out[layer])
        x = layer_norm(DEEPNORM_ALPHA * x + f, ln_g[layer, 1], ln_b[layer, 1])
    return x


_drawn_inputs = setup_inputs


def setup_inputs(seed=0):
    import zlib

    import numpy as np

    out = dict(_drawn_inputs(seed))
    spreads = {}
    factors = {'b_subln_g': 23.923, 'ffn_conv_b': 8.0}
    for name, (base, spread) in spreads.items():
        noise = np.random.default_rng([zlib.crc32(name.encode()), seed]).standard_normal(out[name].shape)
        drawn = base * np.exp(spread * noise) if base else spread * noise
        out[name] = __import__('jax').numpy.asarray(drawn.astype(out[name].dtype))
    for name, factor in factors.items():
        out[name] = (out[name] * factor).astype(out[name].dtype)
    return out
```

```python
import math
from contextlib import ExitStack

import concourse.bass as bass
import numpy as np
from concourse import mybir

F32 = mybir.dt.float32
F32R = mybir.dt.float32r
I32 = mybir.dt.int32
ALU = mybir.AluOpType
ACT = mybir.ActivationFunctionType
AX = mybir.AxisListType

P = 128
RING = 3
CHUNK = 2048
MASKED = -1e30
SUM_EPS = 1e-5
ROPE_THETA = 500000.0
TWO_PI = 2.0 * math.pi
ROUND = 1.5 * 2.0 ** 23


def two_pi_pieces():
    rest, pieces = TWO_PI, []
    for _ in range(3):
        e = math.floor(math.log2(rest)) - 11
        piece = math.floor(rest / 2.0 ** e) * 2.0 ** e
        pieces.append(piece)
        rest -= piece
    return pieces


def mixer_schedule(layer, first_chunk, fills_before):
    items, fills, late = [], [fills_before], []

    def fill():
        fills[0] += 1
        return fills[0] - 1

    def product(item, chunk, ends):
        items.append(item)
        while late:
            items.append(late.pop())
        if ends:
            late.append(("split", chunk + RING))

    def projection(cgs):
        after = {}
        for cg in cgs:
            for kt in range(8):
                yield ("proj", cg, kt), first_chunk + 2 * cg + kt // 4, kt % 4 == 3, after.pop(kt, [])
            after = {3: [("qkT", cg, 0)], 5: [("qkT", cg, 1)]} if cg % 3 < 2 else {}

    def emit(step):
        item, chunk, ends, then = step
        product(item, chunk, ends)
        if item[0] == "proj" and item[2] == 7:
            items.append(("drain", item[1]))
        for t in then:
            items.append(t + (fill(),))

    for step in projection(range(3)):
        emit(step)

    pieces = []
    if layer == 0:
        for m in range(16 + 3):
            if m < 16:
                pieces.append([("scores", m)])
            if 1 <= m <= 16:
                pieces[-1 if m < 16 else len(pieces):] = (
                    [pieces[-1] + [("norm", m - 1)]] if m < 16 else [[("norm", m - 1)]])
            if 2 <= m <= 17:
                pieces.append([("probT", m - 2)])
            if m >= 3:
                pieces.append([("pv", m - 3)] + ([("out", (m - 3) // 2)] if m % 2 == 0 else []))
    else:
        for p in range(8 + 2):
            if p < 8:
                pieces.append([("scores", 2 * p)])
                pieces.append([("scores", 2 * p + 1)])
            if 1 <= p <= 8:
                pieces.append([("norm", p - 1)])
            if p >= 2:
                pieces.append([("outT", p - 2), ("out", p - 2)])
            if 1 <= p <= 8:
                pieces.append([("probT", p - 1)])
                pieces.append([("pv", p - 1), ("subln", p - 1)])

    second = list(projection(range(3, 6)))
    outputs = [(kt, st) for kt in range(8) for st in range(2)]
    ready = {}
    half = next(n for n, piece in enumerate(pieces) if piece[0] == ("scores", 8))
    done, taken = 0, 0
    for n, piece in enumerate(pieces):
        if n < half:
            while done * half < len(second) * n:
                emit(second[done])
                done += 1
        elif n == half:
            while done < len(second):
                emit(second[done])
                done += 1
        else:
            kt, st = outputs[0] if outputs else (8, 0)
            due = (n - half) * 16 >= (len(pieces) - half) * taken
            if due and kt in ready and n >= ready[kt] + 2:
                product(("wo", kt, st), first_chunk + 12 + kt // 2, kt % 2 == 1 and st == 1)
                outputs.pop(0)
                taken += 1
        for item in piece:
            items.append(item + (fill(),) if item[0] == "probT" else item)
            if item[0] == "out":
                ready[item[1]] = n
    for kt, st in outputs:
        product(("wo", kt, st), first_chunk + 12 + kt // 2, kt % 2 == 1 and st == 1)
    assert late == [("split", first_chunk + 15 + RING)]
    return items, fills[0]


def yoco_trunk(nc, x, positions, a_w_qkv, a_w_o, w_kv_shared, b_w_q, b_w_o, b_lambda, b_subln_g,
               ln_g, ln_b, ffn_w_in, ffn_conv_w, ffn_conv_b, ffn_w_out, out):
    SEQ, D = x.shape[1], x.shape[2]
    LAYERS = ln_g.shape[0]
    DFF = ffn_w_out.shape[1]
    ST, KT = SEQ // P, D // P
    FT = DFF // P
    GROUPS = FT // 2
    HALF = D // 2
    ALPHA = (2 * LAYERS) ** 0.25
    SCALE = 64 ** -0.5
    LAMBDA_INIT = 0.8 - 0.6 * math.exp(-0.3 * (LAYERS // 2))
    ROT = 8
    assert (SEQ, D, LAYERS, FT % 2) == (256, 1024, 2, 0)
    QKV_CHUNKS, WO_CHUNKS = 12, 4
    LAYER_CHUNKS = QKV_CHUNKS + WO_CHUNKS + 3 * GROUPS
    CHUNKS = LAYERS * LAYER_CHUNKS
    MAPS = 16

    schedule, fills = [], 0
    for layer in range(LAYERS):
        items, fills = mixer_schedule(layer, layer * LAYER_CHUNKS, fills)
        schedule.append(items)
    fill_of = {(layer,) + it[:-1]: it[-1] for layer, items in enumerate(schedule) for it in items
               if it[0] in ("qkT", "probT")}

    def ffn_chunk(layer, i, which):
        base = layer * LAYER_CHUNKS + QKV_CHUNKS + WO_CHUNKS
        if which == 2:
            return base + 2 + 3 * i + 2 if not isinstance(i, int) or i < GROUPS - 1 else base + 3 * i + 2
        return base + 3 * i - 1 + which if not isinstance(i, int) or i > 0 else base + which

    with ExitStack() as ctx:
        def sb(name, shape, dt=F32):
            return ctx.enter_context(nc.sbuf_tensor(name, shape, dt))

        def sem(name):
            return ctx.enter_context(nc.semaphore(name))

        raw = [sb(f"raw{s}", [P, CHUNK]) for s in range(RING)]
        w_hi = [sb(f"w_hi{s}", [P, CHUNK], F32R) for s in range(RING)]
        w_lo = [sb(f"w_lo{s}", [P, CHUNK], F32R) for s in range(RING)]
        xs = sb("xs", [P, ST, D])
        xT_hi = sb("xT_hi", [P, KT, SEQ], F32R)
        xT_lo = sb("xT_lo", [P, KT, SEQ], F32R)
        rows = [sb("q_rows", [P, ST, HALF]), sb("k_rows", [P, ST, HALF])]
        headT = [sb("qT", [P, KT, SEQ]), sb("kT", [P, KT, SEQ])]
        v_rows = sb("v_rows", [P, ST, D])
        oT_hi = sb("oT_hi", [P, KT, SEQ], F32R)
        oT_lo = sb("oT_lo", [P, KT, SEQ], F32R)
        masked = sb("masked", [P, 2, 3 * P])
        probs = sb("probs", [P, 4, 3 * P])
        probsT = sb("probsT", [P, 2, 3 * P])
        neg_max = sb("neg_max", [P, 4, ST])
        sums = sb("sums", [P, 4, ST])
        recips = sb("recips", [P, 4, ST])
        head_out = sb("head_out", [P, ST, P])
        squares = sb("squares", [P, ST, P])
        mean_sq = sb("mean_sq", [P, 2, ST])
        rms_inv = sb("rms_inv", [P, 2, ST])
        conv = sb("conv", [P, 2, SEQ])
        gelu = sb("gelu", [P, 2, SEQ])
        hidden = sb("hidden", [P, 2, SEQ])
        hT_hi = sb("hT_hi", [P, 2, SEQ], F32R)
        hT_lo = sb("hT_lo", [P, 2, SEQ], F32R)
        gain = sb("gain", [P, 2, D])
        shift = sb("shift", [P, 2, D])
        conv_rows = sb("conv_rows", [4 * FT, LAYERS, P])
        conv_cols = sb("conv_cols", [P, LAYERS, 4 * FT])
        stats = sb("stats", [P, ST, 2, 6])
        moments = sb("moments", [P, ST, 2])
        var_eps = sb("var_eps", [P, ST])
        std_inv = sb("std_inv", [P, ST])
        minus_half = sb("minus_half", [P, ST])
        ident = sb("ident", [P, P])
        causal = sb("causal", [P, 3 * P])
        zeros = sb("zeros", [P, 4 * P], F32R)
        pos_i = sb("pos_i", [P, ST], I32)
        pos_f = sb("pos_f", [P, ST])
        freq = sb("freq", [P, ROT])
        angle = sb("angle", [P, ST, ROT])
        turns = sb("turns", [P, ST, ROT])
        small = sb("small", [P, ST, ROT])
        sines = sb("sines", [P, 2, ST, ROT])
        cos2 = sb("cos2", [P, ST, 2 * ROT])
        sin2 = sb("sin2", [P, ST, 2 * ROT])
        rot_a = sb("rot_a", [P, ST, KT, 2 * ROT])
        rot_b = sb("rot_b", [P, ST, KT, 2 * ROT])
        lam_in = sb("lam_in", [P, 4, 64])
        lam_prod = sb("lam_prod", [P, 2, 64])
        lam_dot = sb("lam_dot", [P, 2])
        lam_exp = sb("lam_exp", [P, 2])
        neg_lam = sb("neg_lam", [P, 1])
        neg_lam_r = sb("neg_lam_r", [P, 2, ST])
        sub_g = sb("sub_g", [P, 1])
        sub_gain = sb("sub_gain", [P, 1])

        def bank(name):
            return ctx.enter_context(nc.psum_tensor(name, [P, 512], F32))

        wide = [bank(f"wide{b}") for b in range(4)]
        score_bank = [bank("score0"), bank("score1")]
        turn_bank = bank("turn")
        out_bank = bank("outb")
        side = [score_bank[0], score_bank[1], turn_bank, out_bank]
        up_bank, gate_bank = side[0:2], side[2:4]

        raw_in = [sem(f"raw_in{s}") for s in range(RING)]
        hi_done, lo_done, chunk_used = sem("hi_done"), sem("lo_done"), sem("chunk_used")
        x_in, small_in, norm_in, out_stored = sem("x_in"), sem("small_in"), sem("norm_in"), sem("out_stored")
        consts_done, tables_done = sem("consts_done"), sem("tables_done")
        angle_done, sines_done, lam_dot_done, lam_exp_done = (
            sem("angle_done"), sem("sines_done"), sem("lam_dot_done"), sem("lam_exp_done"))
        pool_step, act_step, dve_step = sem("pool_step"), sem("act_step"), sem("dve_step")
        xT_filled, xhi_done, xlo_done = sem("xT_filled"), sem("xhi_done"), sem("xlo_done")
        cols_filled, cols_drained = sem("cols_filled"), sem("cols_drained")
        proj_drained, rope_done = sem("proj_drained"), sem("rope_done")
        turn_filled, turn_drained = sem("turn_filled"), sem("turn_drained")
        scores_done, masked_done, max_done, exp_done, norm_done = (
            sem("scores_done"), sem("masked_done"), sem("max_done"), sem("exp_done"), sem("norm_done"))
        pv_done, squares_done, mean_sq_done, rms_done, head_done, headT_done = (
            sem("pv_done"), sem("squares_done"), sem("mean_sq_done"), sem("rms_done"), sem("head_done"),
            sem("headT_done"))
        ohi_done, olo_done = sem("ohi_done"), sem("olo_done")
        y0_done, var_done, std_done, norm_x_done = sem("y0_done"), sem("var_done"), sem("std_done"), sem("norm_x_done")
        up0_done, gate0_done = sem("up0_done"), sem("gate0_done")
        tap_done, conv_done, gelu_done, hidden_done = sem("tap_done"), sem("conv_done"), sem("gelu_done"), sem("hidden_done")
        hhi_done, hlo_done = sem("hhi_done"), sem("hlo_done")

        block = ctx.enter_context(nc.Block())

        @block.sync
        def _(sp):
            sp.dma_start(xs[:, :, :], x[0].rearrange("(t p) d -> p t d", p=P)).then_inc(x_in, 16)

            def load(c, slot, dst, src):
                if not isinstance(c, int) or c >= RING:
                    sp.wait_ge(lo_done, c - RING + 1)
                sp.dma_start(dst(raw[slot][:, :]), src).then_inc(raw_in[slot], 16)

            for layer in range(LAYERS):
                base = layer * LAYER_CHUNKS
                for cg in range(6):
                    g, mat = divmod(cg, 3)
                    if layer == 0:
                        w, col = a_w_qkv[0], mat * D + g * HALF
                    else:
                        w, col = (b_w_q[0], g * HALF) if mat == 0 else (w_kv_shared, (mat - 1) * D + g * HALF)
                    for h in range(2):
                        c = base + 2 * cg + h
                        load(c, c % RING, lambda r: r.rearrange("p (k n) -> p k n", k=4),
                             w[4 * P * h:4 * P * (h + 1), col:col + HALF].rearrange("(k p) n -> p k n", p=P))
                wo = (a_w_o if layer == 0 else b_w_o)[0]
                for t in range(WO_CHUNKS):
                    c = base + QKV_CHUNKS + t
                    load(c, c % RING, lambda r: r.rearrange("p (k n) -> p k n", k=2),
                         wo[2 * P * t:2 * P * (t + 1), :].rearrange("(k p) n -> p k n", p=P))

                w_in = ffn_w_in[layer].rearrange("(k p) n -> p k n", p=P)
                w_out = ffn_w_out[layer].rearrange("(k p) n -> p k n", p=P)

                def load_in(i, which):
                    load(ffn_chunk(layer, i, which), ffn_chunk(layer, 1 if not isinstance(i, int) else i, which) % RING,
                         lambda r: r.rearrange("p (k n) -> p k n", k=KT),
                         w_in[:, :, bass.ds(which * DFF + i * 2 * P, 2 * P)])

                def load_out(i):
                    load(ffn_chunk(layer, i, 2), ffn_chunk(layer, 0 if not isinstance(i, int) else i, 2) % RING,
                         lambda r: r.rearrange("p (k n) -> p k n", k=2), w_out[:, bass.ds(2 * i, 2), :])

                load_in(0, 0)
                load_in(0, 1)
                with sp.Fori(1, GROUPS) as i:
                    load_in(i, 0)
                    load_in(i, 1)
                    load_out(i - 1)
                load_out(GROUPS - 1)
            for st in range(ST):
                sp.wait_ge(norm_x_done, 2 * (2 * LAYERS - 1) + st + 1)
                sp.dma_start(out[0, st * P:(st + 1) * P, :], xs[:, st, :]).then_inc(out_stored, 16)
            sp.wait_ge(out_stored, 16 * ST)

        @block.gpsimd
        def _(pool):
            for st in range(ST):
                pool.dma_start(pos_i[:, st:st + 1], positions[0, st * P:(st + 1) * P].rearrange("(p o) -> p o", o=1)
                               ).then_inc(small_in, 16)
            pool.dma_start(lam_in[:, :, :], bass.AP(tensor=b_lambda.tensor, offset=b_lambda.offset, ap=[[0, P], [64, 4], [1, 64]])
                           ).then_inc(small_in, 16)
            pool.dma_start(sub_g[:, :], b_subln_g[0].rearrange("(p o) -> p o", o=1)).then_inc(small_in, 16)
            for layer in range(LAYERS):
                pool.dma_start(conv_rows[0:3 * FT, layer, :],
                               ffn_conv_w[layer].rearrange("t (j p) -> (t j) p", p=P)).then_inc(small_in, 16)
                pool.dma_start(conv_rows[3 * FT:4 * FT, layer, :],
                               ffn_conv_b[layer].rearrange("(j p) -> j p", p=P)).then_inc(small_in, 16)
            nc.gpsimd.memset(ident[:, :], 0.0).then_inc(pool_step, 1)
            pool.wait_ge(pool_step, 1)
            nc.gpsimd.affine_select(ident[:, :], ident[:, :], pattern=[[-1, P]], compare_op=ALU.not_equal,
                                    fill=1.0, base=0, channel_multiplier=1).then_inc(consts_done, 1)
            for r in range(ROT):
                inv = 1.0 / np.float32(ROPE_THETA) ** np.float32(r * 2.0 / (2 * ROT))
                nc.gpsimd.memset(freq[:, r:r + 1], float(np.float32(inv))).then_inc(consts_done, 1)
            nc.gpsimd.memset(minus_half[:, :], -0.5)
            nc.gpsimd.memset(zeros[:, :].bitcast(F32), 0.0)
            nc.gpsimd.memset(causal[:, :], 0.0).then_inc(pool_step, 1)
            pool.wait_ge(pool_step, 2)
            for b in (0, 2):
                nc.gpsimd.affine_select(causal[:, b * P:(b + 1) * P], causal[:, b * P:(b + 1) * P],
                                        pattern=[[-1, P]], compare_op=ALU.is_ge, fill=MASKED, base=0,
                                        channel_multiplier=1).then_inc(consts_done, 1)
            pool.wait_ge(lo_done, RING)
            for n in range(2 * LAYERS):
                if n % 2 == 0:
                    if n:
                        pool.wait_ge(norm_x_done, 2 * n)
                    for tile, src in ((gain, ln_g), (shift, ln_b)):
                        pool.dma_start(tile[:, :, :], bass.AP(tensor=src.tensor, offset=src.offset + n * D,
                                                              ap=[[0, P], [D, 2], [1, D]])).then_inc(norm_in, 16)
                if n == 2:
                    for p in range(MAPS // 2):
                        pool.wait_ge(mean_sq_done, p + 1)
                        nc.gpsimd.tensor_tensor(rms_inv[:, p % 2, :], mean_sq[:, p % 2, :], minus_half[:, :],
                                                ALU.pow).then_inc(rms_done, 1)
                for st in range(ST):
                    pool.wait_ge(var_done, ST * n + st + 1)
                    nc.gpsimd.tensor_tensor(std_inv[:, st:st + 1], var_eps[:, st:st + 1], minus_half[:, 0:1],
                                            ALU.pow).then_inc(std_done, 1)

        @block.scalar
        def _(act):
            def split_hi(c, slot, round_of):
                act.wait_ge(raw_in[slot], round_of)
                if not isinstance(c, int) or c >= RING:
                    act.wait_ge(chunk_used, c - RING + 1)
                nc.scalar.activation(w_hi[slot][:, :], raw[slot][:, :], ACT.Copy).then_inc(hi_done, 1)

            def split_static(c):
                if c < CHUNKS:
                    split_hi(c, c % RING, 16 * (c // RING + 1))

            def xT_hi_part(n):
                for f in range(4):
                    act.wait_ge(xT_filled, 4 * n + f + 1)
                    st, half = divmod(f, 2)
                    nc.scalar.activation(xT_hi[:, 4 * half:4 * half + 4, st * P:(st + 1) * P],
                                         side[f][:, :].rearrange("p (k q) -> p k q", k=4),
                                         ACT.Copy).then_inc(xhi_done, 1)

            xT_hi_part(0)
            for c in range(RING):
                split_static(c)
            act.wait_ge(angle_done, 1)
            nc.scalar.activation(sines[:, 0], angle[:, :, :], ACT.Sin)
            nc.scalar.activation(sines[:, 1], angle[:, :, :], ACT.Sin, scale=0.5).then_inc(sines_done, 1)
            act.wait_ge(lam_dot_done, 1)
            nc.scalar.activation(lam_exp[:, :], lam_dot[:, :], ACT.Exp).then_inc(lam_exp_done, 1)
            for layer in range(LAYERS):
                act.wait_ge(cols_filled, LAYERS)
                nc.scalar.activation(conv_cols[:, layer, :], out_bank[:, 4 * FT * layer:4 * FT * (layer + 1)],
                                     ACT.Copy).then_inc(cols_drained, 1)

            for layer in range(LAYERS):
                base = layer * LAYER_CHUNKS
                for item in schedule[layer]:
                    kind, m = item[0], item[1]
                    if kind == "split":
                        split_static(m)
                    elif kind == "drain":
                        g, mat = divmod(m, 3)
                        act.wait_ge(chunk_used, base + 2 * m + 2)
                        if mat < 2 and (layer, g) != (0, 0):
                            before = (layer, "qkT", m - 3, 1) if g else (layer - 1, "qkT", m + 3, 1)
                            act.wait_ge(turn_filled, fill_of[before] + 1)
                        for st in range(ST):
                            dst = rows[mat][:, st, :] if mat < 2 else v_rows[:, st, g * HALF:(g + 1) * HALF]
                            nc.scalar.activation(dst, wide[2 * (m % 2) + st][:, :], ACT.Copy).then_inc(proj_drained, 1)
                    elif kind == "qkT":
                        _, cg, f, n = item
                        g, mat = divmod(cg, 3)
                        act.wait_ge(turn_filled, n + 1)
                        nc.scalar.activation(headT[mat][:, 4 * g + 2 * f:4 * g + 2 * f + 2, :],
                                             turn_bank[:, :].rearrange("p (k q) -> p k q", k=2),
                                             ACT.Copy).then_inc(turn_drained, 1)
                    elif kind == "scores":
                        j = MAPS * layer + m
                        act.wait_ge(max_done, j + 1)
                        if layer == 0 and m >= 4:
                            act.wait_ge(turn_filled, fill_of[(0, "probT", m - 4)] + 1)
                        elif layer == 1:
                            before = (1, "probT", m // 2 - 2) if m >= 4 else (0, "probT", MAPS - 4 + m)
                            act.wait_ge(turn_filled, fill_of[before] + 1)
                        for q, (lo, hi) in enumerate(((0, P), (P, 3 * P))):
                            last = nc.scalar.activation(probs[:, m % 4, lo:hi], masked[:, m % 2, lo:hi], ACT.Exp,
                                                        bias=neg_max[:, m % 4, q:q + 1],
                                                        accum_out=sums[:, m % 4, q:q + 1])
                        last.then_inc(exp_done, 1)
                    elif kind == "probT":
                        n = item[-1]
                        act.wait_ge(turn_filled, n + 1)
                        if layer == 0 and m >= 2:
                            act.wait_ge(pv_done, m - 1)
                        elif layer == 1:
                            act.wait_ge(pv_done, MAPS + m - 1)
                        nc.scalar.activation(probsT[:, m % 2, :], turn_bank[:, 0:3 * P], ACT.Copy).then_inc(turn_drained, 1)
                    elif kind == "subln":
                        act.wait_ge(pv_done, MAPS + m + 1)
                        if m >= 2:
                            act.wait_ge(mean_sq_done, m - 1)
                        for st in range(ST):
                            last = nc.scalar.activation(squares[:, st, :], out_bank[:, st * P:(st + 1) * P], ACT.Square,
                                                        accum_out=mean_sq[:, m % 2, st:st + 1])
                        last.then_inc(squares_done, 1)
                    elif kind == "out":
                        if layer == 0:
                            act.wait_ge(pv_done, 2 * m + 2)
                            nc.scalar.activation(oT_hi[:, m, :], out_bank[:, 0:SEQ], ACT.Copy).then_inc(ohi_done, 1)
                        else:
                            act.wait_ge(headT_done, m + 1)
                            nc.scalar.activation(oT_hi[:, m, :], out_bank[:, SEQ:2 * SEQ], ACT.Copy,
                                                 scale=sub_gain[:, 0:1]).then_inc(ohi_done, 1)
                xT_hi_part(2 * layer + 1)
                split_static(base + QKV_CHUNKS + WO_CHUNKS - 1 + RING)

                def ffn_group(i, peeled):
                    t = GROUPS * layer + i
                    cu, cg = ffn_chunk(layer, i, 0), ffn_chunk(layer, i, 1)
                    at = 1 if peeled == "loop" else i
                    slot_u, slot_g = ffn_chunk(layer, at, 0) % RING, ffn_chunk(layer, at, 1) % RING

                    def split_after(c, slot):
                        if peeled == "loop":
                            first = ffn_chunk(layer, 1, 0) + {slot_u: 0, slot_g: 1}.get(slot, 2) + RING
                            split_hi(c + RING, slot, 16 * (first // RING + 1) + 16 * (i - 1))
                        else:
                            split_static(c + RING)

                    for tt in range(2):
                        if tt == 0:
                            act.wait_ge(up0_done, t + 1)
                        else:
                            act.wait_ge(chunk_used, cu + 1)
                        nc.scalar.activation(conv[:, tt, :], up_bank[tt][:, 0:SEQ], ACT.Identity,
                                             scale=conv_cols[:, layer, bass.ds(2 * FT + 2 * i + tt, 1)],
                                             bias=conv_cols[:, layer, bass.ds(3 * FT + 2 * i + tt, 1)]
                                             ).then_inc(tap_done, 1)
                    for tt in range(2):
                        act.wait_ge(conv_done, 2 * t + tt + 1)
                        if peeled == "loop" or t > 0:
                            act.wait_ge(hidden_done, 2 * t + tt - 1)
                        nc.scalar.activation(gelu[:, tt, :], conv[:, tt, :], ACT.Gelu_apprx_tanh).then_inc(gelu_done, 1)
                    split_after(cu, slot_u)
                    if peeled != "last":
                        split_after(cg, slot_g)
                    for tt in range(2):
                        act.wait_ge(hidden_done, 2 * t + tt + 1)
                        if tt == 0 and peeled != "first":
                            act.wait_ge(chunk_used, ffn_chunk(layer, i, 1) + 2)
                        nc.scalar.activation(hT_hi[:, tt, :], hidden[:, tt, :], ACT.Copy).then_inc(hhi_done, 1)
                    if peeled == "last":
                        split_after(cg, slot_g)
                    if peeled != "first":
                        split_after(cg + 1, (slot_g + 1) % RING)

                ffn_group(0, "first")
                with act.Fori(1, GROUPS - 1) as i:
                    ffn_group(i, "loop")
                ffn_group(GROUPS - 1, "last")
                if layer + 1 < LAYERS:
                    xT_hi_part(2 * layer + 2)
                split_static(base + LAYER_CHUNKS - 1 + RING)

        @block.vector
        def _(dve):
            steps = {"n": 0, "i": None, "from": 0, "per": 0}

            def link(ins):
                steps["n"] += 1
                ins.then_inc(dve_step, 1)
                if steps["i"] is None:
                    dve.wait_ge(dve_step, steps["n"])
                else:
                    dve.wait_ge(dve_step, steps["n"] + (steps["i"] - 1) * steps["per"])

            def split_lo(c, slot):
                dve.wait_ge(hi_done, c + 1)
                nc.vector.tensor_tensor(w_lo[slot][:, :], raw[slot][:, :], w_hi[slot][:, :].bitcast(F32),
                                        ALU.subtract).then_inc(lo_done, 1)

            def split_static(c):
                if c < CHUNKS:
                    split_lo(c, c % RING)

            def xT_lo_part(n):
                for f in range(4):
                    dve.wait_ge(xhi_done, 4 * n + f + 1)
                    st, half = divmod(f, 2)
                    part = (slice(None), slice(4 * half, 4 * half + 4), slice(st * P, (st + 1) * P))
                    nc.vector.tensor_tensor(xT_lo[part], side[f][:, :].rearrange("p (k q) -> p k q", k=4),
                                            xT_hi[part].bitcast(F32), ALU.subtract).then_inc(xlo_done, 1)

            def layer_norm(n):
                for st in range(ST):
                    if st == 0:
                        dve.wait_ge(y0_done, n + 1)
                    else:
                        dve.wait_ge(chunk_used, (n // 2) * LAYER_CHUNKS + (QKV_CHUNKS + WO_CHUNKS if n % 2 == 0
                                                                           else LAYER_CHUNKS))
                    for half in range(2):
                        part = xs[:, st, half * HALF:(half + 1) * HALF]
                        last = nc.vector.scalar_tensor_tensor(part, part, ALPHA, wide[2 * st + half][:, :],
                                                              ALU.mult, ALU.add)
                    link(last)
                    for half in range(2):
                        last = nc.vector.bn_stats(stats[:, st, half, :], xs[:, st, half * HALF:(half + 1) * HALF])
                    link(last)
                    link(nc.vector.bn_aggr(moments[:, st, :], stats[:, st, :, :].rearrange("p a b -> p (a b)")))
                    nc.vector.tensor_scalar(var_eps[:, st:st + 1], moments[:, st, 1:2], SUM_EPS, None,
                                            ALU.add).then_inc(var_done, 1)
                    dve.wait_ge(std_done, ST * n + st + 1)
                    link(nc.vector.tensor_scalar(xs[:, st, :], xs[:, st, :], moments[:, st, 0:1],
                                                 std_inv[:, st:st + 1], ALU.subtract, ALU.mult))
                    if st == 0:
                        dve.wait_ge(norm_in, 32 * (n // 2 + 1))
                    link(nc.vector.tensor_tensor(xs[:, st, :], xs[:, st, :], gain[:, n % 2, :], ALU.mult))
                    nc.vector.tensor_tensor(xs[:, st, :], xs[:, st, :], shift[:, n % 2, :],
                                            ALU.add).then_inc(norm_x_done, 1)

            xT_lo_part(0)
            for c in range(RING):
                split_static(c)

            dve.wait_ge(small_in, 16 * 8)
            dve.wait_ge(consts_done, 1 + ROT)
            link(nc.vector.tensor_copy(pos_f[:, :], pos_i[:, :]))
            for st in range(ST):
                last = nc.vector.tensor_scalar(angle[:, st, :], freq[:, :], pos_f[:, st:st + 1], None, ALU.mult)
            link(last)
            pieces = two_pi_pieces()
            link(nc.vector.memset(small[:, :, :], 0.0))
            for times in (4096.0, 1.0):
                link(nc.vector.tensor_scalar(turns[:, :, :], angle[:, :, :], 1.0 / (TWO_PI * times), None, ALU.mult))
                link(nc.vector.tensor_scalar(turns[:, :, :], turns[:, :, :], ROUND, None, ALU.add))
                link(nc.vector.tensor_scalar(turns[:, :, :], turns[:, :, :], ROUND, None, ALU.subtract))
                for n, piece in enumerate(pieces):
                    into = angle if n < 2 else small
                    link(nc.vector.scalar_tensor_tensor(into[:, :, :], turns[:, :, :], -piece * times,
                                                        into[:, :, :], ALU.mult, ALU.add))
            link(nc.vector.tensor_tensor(angle[:, :, :], angle[:, :, :], small[:, :, :], ALU.add))
            link(nc.vector.tensor_scalar(turns[:, :, :], angle[:, :, :], 1.0 / TWO_PI, None, ALU.mult))
            link(nc.vector.tensor_scalar(turns[:, :, :], turns[:, :, :], ROUND, None, ALU.add))
            link(nc.vector.tensor_scalar(turns[:, :, :], turns[:, :, :], ROUND, None, ALU.subtract))
            for piece in (pieces[0], TWO_PI - pieces[0]):
                link(nc.vector.scalar_tensor_tensor(angle[:, :, :], turns[:, :, :], -piece, angle[:, :, :],
                                                    ALU.mult, ALU.add))
            nc.vector.tensor_scalar(angle[:, :, :], angle[:, :, :], 3.1415925, -3.1415925, ALU.min,
                                    ALU.max).then_inc(angle_done, 1)
            link(nc.vector.tensor_tensor(lam_prod[:, :, :], lam_in[:, :, :].rearrange("p (a b) d -> p a b d", b=2)[:, :, 0, :],
                                         lam_in[:, :, :].rearrange("p (a b) d -> p a b d", b=2)[:, :, 1, :], ALU.mult))
            nc.vector.tensor_reduce(lam_dot[:, :], lam_prod[:, :, :], AX.X, ALU.add).then_inc(lam_dot_done, 1)
            nc.vector.tensor_scalar(sub_gain[:, :], sub_g[:, :], 1.0 - LAMBDA_INIT, None, ALU.mult)
            dve.wait_ge(sines_done, 1)
            link(nc.vector.tensor_tensor(small[:, :, :], sines[:, 1], sines[:, 1], ALU.mult))
            for h in range(2):
                nc.vector.tensor_scalar(cos2[:, :, h * ROT:(h + 1) * ROT], small[:, :, :], -2.0, 1.0, ALU.mult, ALU.add)
                last = nc.vector.tensor_scalar(sin2[:, :, h * ROT:(h + 1) * ROT], sines[:, 0], 2.0 * h - 1.0, None,
                                               ALU.mult)
            link(last)
            dve.wait_ge(lam_exp_done, 1)
            link(nc.vector.tensor_tensor(neg_lam[:, :], lam_exp[:, 1:2], lam_exp[:, 0:1], ALU.subtract))
            link(nc.vector.tensor_scalar(neg_lam[:, :], neg_lam[:, :], LAMBDA_INIT, None, ALU.subtract))
            dve.wait_ge(consts_done, 3 + ROT)

            for layer in range(LAYERS):
                base = layer * LAYER_CHUNKS
                for item in schedule[layer]:
                    kind, m = item[0], item[1]
                    if kind == "split":
                        split_static(m)
                    elif kind == "drain" and m % 3 < 2:
                        dve.wait_ge(proj_drained, 12 * layer + 2 * m + 2)
                        for st in range(ST):
                            heads = rows[m % 3][:, st, :].rearrange("p (h d) -> p h d", d=64)

                            def over_heads(table, a, b):
                                return table[:, st, a:b].unsqueeze(1).broadcast_to([P, KT, b - a])

                            nc.vector.tensor_tensor(rot_a[:, st], heads[:, :, 0:2 * ROT],
                                                    over_heads(cos2, 0, 2 * ROT), ALU.mult)
                            nc.vector.tensor_tensor(rot_b[:, st, :, 0:ROT], heads[:, :, ROT:2 * ROT],
                                                    over_heads(sin2, 0, ROT), ALU.mult)
                            last = nc.vector.tensor_tensor(rot_b[:, st, :, ROT:2 * ROT], heads[:, :, 0:ROT],
                                                           over_heads(sin2, ROT, 2 * ROT), ALU.mult)
                        link(last)
                        for st in range(ST):
                            heads = rows[m % 3][:, st, :].rearrange("p (h d) -> p h d", d=64)
                            last = nc.vector.tensor_tensor(heads[:, :, 0:2 * ROT], rot_a[:, st], rot_b[:, st], ALU.add)
                        last.then_inc(rope_done, 1)
                    elif kind == "scores":
                        j = MAPS * layer + m
                        dve.wait_ge(scores_done, j + 1)
                        if j >= 2:
                            dve.wait_ge(exp_done, j - 1)
                        nc.vector.scalar_tensor_tensor(masked[:, m % 2, :], score_bank[m % 2][:, 0:3 * P], SCALE,
                                                       causal[:, :], ALU.mult, ALU.add).then_inc(masked_done, 1)
                        dve.wait_ge(masked_done, j + 1)
                        for q, (lo, hi) in enumerate(((0, P), (P, 3 * P))):
                            last = nc.vector.tensor_reduce(neg_max[:, m % 4, q:q + 1], masked[:, m % 2, lo:hi], AX.X,
                                                           ALU.max, negate=True)
                        last.then_inc(max_done, 1)
                    elif kind == "norm" and layer == 0:
                        dve.wait_ge(exp_done, m + 1)
                        link(nc.vector.reciprocal(recips[:, m % 4, :], sums[:, m % 4, :]))
                        for q, (lo, hi) in enumerate(((0, P), (P, 3 * P))):
                            last = nc.vector.tensor_scalar(probs[:, m % 4, lo:hi], probs[:, m % 4, lo:hi],
                                                           recips[:, m % 4, q:q + 1], None, ALU.mult)
                        last.then_inc(norm_done, 1)
                    elif kind == "norm":
                        a = 2 * (m % 2)
                        dve.wait_ge(exp_done, MAPS + 2 * m + 2)
                        link(nc.vector.reciprocal(recips[:, a:a + 2, :], sums[:, a:a + 2, :]))
                        link(nc.vector.tensor_scalar(neg_lam_r[:, m % 2, :], recips[:, a + 1, :], neg_lam[:, 0:1],
                                                     None, ALU.mult))
                        for q, (lo, hi) in enumerate(((0, P), (P, 3 * P))):
                            last = nc.vector.tensor_scalar(probs[:, a + 1, lo:hi], probs[:, a + 1, lo:hi],
                                                           neg_lam_r[:, m % 2, q:q + 1], None, ALU.mult)
                        link(last)
                        for q, (lo, hi) in enumerate(((0, P), (P, 3 * P))):
                            last = nc.vector.scalar_tensor_tensor(probs[:, a, lo:hi], probs[:, a, lo:hi],
                                                                  recips[:, a, q:q + 1], probs[:, a + 1, lo:hi],
                                                                  ALU.mult, ALU.add)
                        last.then_inc(norm_done, 1)
                    elif kind == "subln":
                        dve.wait_ge(squares_done, m + 1)
                        nc.vector.tensor_scalar(mean_sq[:, m % 2, :], mean_sq[:, m % 2, :], 1.0 / P, SUM_EPS, ALU.mult,
                                                ALU.add).then_inc(mean_sq_done, 1)
                        dve.wait_ge(rms_done, m + 1)
                        if m >= 1:
                            dve.wait_ge(headT_done, m)
                        for st in range(ST):
                            last = nc.vector.tensor_scalar(head_out[:, st, :], out_bank[:, st * P:(st + 1) * P],
                                                           rms_inv[:, m % 2, st:st + 1], None, ALU.mult)
                        last.then_inc(head_done, 1)
                    elif kind == "out":
                        dve.wait_ge(ohi_done, 8 * layer + m + 1)
                        if layer == 0:
                            nc.vector.tensor_tensor(oT_lo[:, m, :], out_bank[:, 0:SEQ], oT_hi[:, m, :].bitcast(F32),
                                                    ALU.subtract).then_inc(olo_done, 1)
                        else:
                            nc.vector.scalar_tensor_tensor(oT_lo[:, m, :], out_bank[:, SEQ:2 * SEQ], sub_gain[:, 0:1],
                                                           oT_hi[:, m, :].bitcast(F32), ALU.mult,
                                                           ALU.subtract).then_inc(olo_done, 1)
                layer_norm(2 * layer)
                xT_lo_part(2 * layer + 1)
                split_static(base + QKV_CHUNKS + WO_CHUNKS - 1 + RING)

                def ffn_group(i, peeled):
                    t = GROUPS * layer + i
                    cu, cg = ffn_chunk(layer, i, 0), ffn_chunk(layer, i, 1)
                    at = 1 if peeled == "loop" else i
                    slot_u, slot_g = ffn_chunk(layer, at, 0) % RING, ffn_chunk(layer, at, 1) % RING

                    def split_after(c, slot):
                        if peeled == "loop":
                            split_lo(c + RING, slot)
                        else:
                            split_static(c + RING)

                    for tt in range(2):
                        dve.wait_ge(tap_done, 2 * t + tt + 1)
                        link(nc.vector.scalar_tensor_tensor(conv[:, tt, 1:SEQ], up_bank[tt][:, 0:SEQ - 1],
                                                            conv_cols[:, layer, bass.ds(FT + 2 * i + tt, 1)],
                                                            conv[:, tt, 1:SEQ], ALU.mult, ALU.add))
                        nc.vector.scalar_tensor_tensor(conv[:, tt, 2:SEQ], up_bank[tt][:, 0:SEQ - 2],
                                                       conv_cols[:, layer, bass.ds(2 * i + tt, 1)],
                                                       conv[:, tt, 2:SEQ], ALU.mult, ALU.add).then_inc(conv_done, 1)
                    split_after(cu, slot_u)
                    for tt in range(2):
                        dve.wait_ge(gelu_done, 2 * t + tt + 1)
                        if tt == 0:
                            dve.wait_ge(gate0_done, t + 1)
                        else:
                            dve.wait_ge(chunk_used, cg + 1)
                        if peeled == "loop" or t > 0:
                            dve.wait_ge(hhi_done, 2 * t + tt - 1)
                        nc.vector.tensor_tensor(hidden[:, tt, :], gelu[:, tt, :], gate_bank[tt][:, 0:SEQ],
                                                ALU.mult).then_inc(hidden_done, 1)
                    if peeled != "last":
                        split_after(cg, slot_g)
                    for tt in range(2):
                        dve.wait_ge(hhi_done, 2 * t + tt + 1)
                        nc.vector.tensor_tensor(hT_lo[:, tt, :], hidden[:, tt, :], hT_hi[:, tt, :].bitcast(F32),
                                                ALU.subtract).then_inc(hlo_done, 1)
                    if peeled == "last":
                        split_after(cg, slot_g)
                    if peeled != "first":
                        split_after(cg + 1, (slot_g + 1) % RING)

                ffn_group(0, "first")
                before = steps["n"]
                LINKS = 2
                with dve.Fori(1, GROUPS - 1) as i:
                    steps["i"], steps["per"] = i, LINKS
                    ffn_group(i, "loop")
                assert steps["n"] == before + LINKS
                steps["n"], steps["i"] = before + LINKS * (GROUPS - 2), None
                ffn_group(GROUPS - 1, "last")
                layer_norm(2 * layer + 1)
                if layer + 1 < LAYERS:
                    xT_lo_part(2 * layer + 2)
                split_static(base + LAYER_CHUNKS - 1 + RING)

        @block.tensor
        def _(pe):
            def product(dst, a_hi, a_lo, b_hi, b_lo, start, stop):
                nc.tensor.matmul(dst, a_hi, b_hi, start=start, stop=False, skip_group_check=True)
                nc.tensor.matmul(dst, a_hi, b_lo, start=False, stop=False, skip_group_check=True)
                return nc.tensor.matmul(dst, a_lo, b_hi, start=False, stop=stop, skip_group_check=True)

            def x_transposes(n):
                for f in range(4):
                    st, half = divmod(f, 2)
                    if n == 0:
                        if f == 0:
                            pe.wait_ge(x_in, 16)
                            pe.wait_ge(consts_done, 1)
                    elif half == 0:
                        pe.wait_ge(norm_x_done, 2 * (n - 1) + st + 1)
                    for k in range(4):
                        last = nc.tensor.transpose(side[f][:, k * P:(k + 1) * P],
                                                   xs[:, st, (4 * half + k) * P:(4 * half + k + 1) * P], ident[:, :])
                    last.then_inc(xT_filled, 1)

            x_transposes(0)
            pe.wait_ge(small_in, 16 * 8)
            pe.wait_ge(xlo_done, 4)
            for layer in range(LAYERS):
                nc.tensor.transpose(out_bank[:, 4 * FT * layer:4 * FT * (layer + 1)], conv_rows[:, layer, :],
                                    ident[0:4 * FT, 0:4 * FT]).then_inc(cols_filled, 1)

            for layer in range(LAYERS):
                base = layer * LAYER_CHUNKS
                pe.wait_ge(xlo_done, 8 * layer + 4)
                for item in schedule[layer]:
                    kind, m = item[0], item[1]
                    j = MAPS * layer + m
                    if kind == "proj":
                        _, cg, kt = item
                        c = base + 2 * cg + kt // 4
                        if kt % 4 == 0:
                            pe.wait_ge(lo_done, c + 1)
                        if kt == 0 and cg >= 2:
                            pe.wait_ge(proj_drained, 12 * layer + 2 * cg - 2)
                        cols = slice((kt % 4) * HALF, (kt % 4 + 1) * HALF)
                        for st in range(ST):
                            rs = slice(st * P, (st + 1) * P)
                            last = product(wide[2 * (cg % 2) + st][:, :], xT_hi[:, kt, rs], xT_lo[:, kt, rs],
                                           w_hi[c % RING][:, cols], w_lo[c % RING][:, cols], kt == 0, kt == KT - 1)
                        if kt % 4 == 3:
                            last.then_inc(chunk_used, 1)
                    elif kind == "qkT":
                        _, cg, f, n = item
                        g, mat = divmod(cg, 3)
                        if f == 0:
                            pe.wait_ge(rope_done, 4 * layer + 2 * g + mat + 1)
                        if n:
                            pe.wait_ge(turn_drained, n)
                        for k in range(2):
                            for st in range(ST):
                                last = nc.tensor.transpose(turn_bank[:, (2 * k + st) * P:(2 * k + st + 1) * P],
                                                           rows[mat][:, st, (2 * f + k) * P:(2 * f + k + 1) * P],
                                                           ident[:, :])
                        last.then_inc(turn_filled, 1)
                    elif kind == "scores":
                        half = slice(64 * (m % 2), 64 * (m % 2) + 64)
                        qT, kT = headT[0][half, m // 2, :], headT[1][half, m // 2, :]
                        if m % 4 == 0:
                            g, f = m // 8, m // 4 % 2
                            pe.wait_ge(turn_drained, fill_of[(layer, "qkT", 3 * g + 1, f)] + 1)
                        if layer == 0 and m == 0:
                            pe.wait_ge(cols_drained, LAYERS)
                        if j >= 2:
                            pe.wait_ge(masked_done, j - 1)
                        bank_ = score_bank[m % 2]
                        nc.tensor.matmul(bank_[:, 0:P], qT[:, 0:P], kT[:, 0:P], start=True, stop=True)
                        nc.tensor.matmul(bank_[:, P:3 * P], qT[:, P:2 * P], kT[:, :], start=True,
                                         stop=True).then_inc(scores_done, 1)
                    elif kind == "probT":
                        n = item[-1]
                        slot = m % 4 if layer == 0 else 2 * (m % 2)
                        pe.wait_ge(norm_done, (0 if layer == 0 else MAPS) + m + 1)
                        pe.wait_ge(turn_drained, n)
                        for b in range(3):
                            last = nc.tensor.transpose(turn_bank[:, b * P:(b + 1) * P], probs[:, slot, b * P:(b + 1) * P],
                                                       ident[:, :])
                        last.then_inc(turn_filled, 1)
                    elif kind == "pv":
                        pe.wait_ge(turn_drained, fill_of[(layer, "probT", m)] + 1)
                        if layer == 0 and m % 8 == 0 or layer == 1 and m % 4 == 0:
                            g = m // 8 if layer == 0 else m // 4
                            pe.wait_ge(proj_drained, 12 * layer + 6 * g + 6)
                        pT = probsT[:, m % 2, :]
                        if layer == 0:
                            if m % 2 == 0 and m >= 2:
                                pe.wait_ge(olo_done, m // 2)
                            part = out_bank[64 * (m % 2):64 * (m % 2) + 64, :]
                            nc.tensor.matmul(part[:, 0:SEQ], v_rows[:, 0, 64 * m:64 * m + 64], pT[:, 0:SEQ], start=True,
                                             stop=False)
                            nc.tensor.matmul(part[:, P:SEQ], v_rows[:, 1, 64 * m:64 * m + 64], pT[:, SEQ:3 * P],
                                             start=False, stop=True).then_inc(pv_done, 1)
                        else:
                            pe.wait_ge(olo_done, 8 + m)
                            v = [v_rows[:, st, P * m:P * (m + 1)] for st in range(ST)]
                            nc.tensor.matmul(out_bank[:, 0:P], pT[:, 0:P], v[0], start=True, stop=True)
                            nc.tensor.matmul(out_bank[:, P:SEQ], pT[:, P:SEQ], v[0], start=True, stop=False)
                            nc.tensor.matmul(out_bank[:, P:SEQ], pT[:, SEQ:3 * P], v[1], start=False,
                                             stop=True).then_inc(pv_done, 1)
                    elif kind == "outT":
                        pe.wait_ge(head_done, m + 1)
                        for st in range(ST):
                            last = nc.tensor.transpose(out_bank[:, SEQ + st * P:SEQ + (st + 1) * P], head_out[:, st, :],
                                                       ident[:, :])
                        last.then_inc(headT_done, 1)
                    elif kind == "wo":
                        _, kt, st = item
                        c = base + QKV_CHUNKS + kt // 2
                        if st == 0:
                            pe.wait_ge(olo_done, 8 * layer + kt + 1)
                            if kt % 2 == 0:
                                pe.wait_ge(lo_done, c + 1)
                            if kt == 0:
                                pe.wait_ge(proj_drained, 12 * layer + 12)
                        rs = slice(st * P, (st + 1) * P)
                        for half in range(2):
                            cols = slice((2 * (kt % 2) + half) * HALF, (2 * (kt % 2) + half + 1) * HALF)
                            last = product(wide[2 * st + half][:, :], oT_hi[:, kt, rs], oT_lo[:, kt, rs],
                                           w_hi[c % RING][:, cols], w_lo[c % RING][:, cols], kt == 0, kt == KT - 1)
                        if st == 1 and kt % 2 == 1:
                            last.then_inc(chunk_used, 1)
                        elif kt == KT - 1:
                            last.then_inc(y0_done, 1)

                x_transposes(2 * layer + 1)
                for b in range(4):
                    nc.tensor.matmul(wide[b][:, :], zeros[:, 0:P], zeros[:, :], start=True, stop=True)
                pe.wait_ge(xlo_done, 8 * layer + 8)

                def features(banks, slot, free, done0):
                    for tt in range(2):
                        if free is not None:
                            pe.wait_ge(*free[tt])
                        for kt in range(KT):
                            cols = slice(kt * 2 * P + tt * P, kt * 2 * P + (tt + 1) * P)
                            last = product(banks[tt][:, 0:SEQ], w_hi[slot][:, cols], w_lo[slot][:, cols],
                                           xT_hi[:, kt, :], xT_lo[:, kt, :], kt == 0, kt == KT - 1)
                        last.then_inc(done0 if tt == 0 else chunk_used, 1)

                def second_product(i, slot, final):
                    pe.wait_ge(lo_done, ffn_chunk(layer, i, 2) + 1 if isinstance(i, int)
                               else layer * LAYER_CHUNKS + QKV_CHUNKS + WO_CHUNKS + 4 + 3 * i + 1)
                    pe.wait_ge(hlo_done, 2 * (GROUPS * layer + i) + 2)
                    for st in range(ST):
                        rs = slice(st * P, (st + 1) * P)
                        for tt in range(2):
                            for half in range(2):
                                cols = slice((2 * tt + half) * HALF, (2 * tt + half + 1) * HALF)
                                last = product(wide[2 * st + half][:, :], hT_hi[:, tt, rs], hT_lo[:, tt, rs],
                                               w_hi[slot][:, cols], w_lo[slot][:, cols], False, final and tt == 1)
                        if st == 1:
                            last.then_inc(chunk_used, 1)
                        elif final:
                            last.then_inc(y0_done, 1)

                def ffn_group(i, peeled):
                    t = GROUPS * layer + i
                    at = 1 if peeled == "loop" else i
                    first = peeled == "first"
                    pe.wait_ge(lo_done, ffn_chunk(layer, i, 0) + 1)
                    features(up_bank, ffn_chunk(layer, at, 0) % RING,
                             None if first else [(conv_done, 2 * t - 1), (conv_done, 2 * t)], up0_done)
                    pe.wait_ge(lo_done, ffn_chunk(layer, i, 1) + 1)
                    features(gate_bank, ffn_chunk(layer, at, 1) % RING,
                             None if first else [(hidden_done, 2 * t - 1), (hidden_done, 2 * t)], gate0_done)
                    if not first:
                        second_product(i - 1, (ffn_chunk(layer, at, 1) + 1) % RING, False)

                ffn_group(0, "first")
                with pe.Fori(1, GROUPS - 1) as i:
                    ffn_group(i, "loop")
                ffn_group(GROUPS - 1, "last")
                second_product(GROUPS - 1, ffn_chunk(layer, GROUPS - 1, 2) % RING, True)
                if layer + 1 < LAYERS:
                    x_transposes(2 * layer + 2)


_INS = ["x", "positions", "a_w_qkv", "a_w_o", "w_kv_shared", "b_w_q", "b_w_o", "b_lambda", "b_subln_g", "ln_g",
        "ln_b", "ffn_w_in", "ffn_conv_w", "ffn_conv_b", "ffn_w_out"]


def kernel(**inputs):
    from concourse import bacc
    from concourse.bass_utils import run_bass_kernel_spmd

    nc = bacc.Bacc("TRN2", target_bir_lowering=False, num_devices=1)
    arrays, args = {}, []
    for name in _INS:
        a = np.ascontiguousarray(inputs[name])
        arrays[f"in_{name}"] = a
        args.append(nc.dram_tensor(f"in_{name}", a.shape, mybir.dt.from_np(a.dtype), kind="ExternalInput").ap())
    shape = inputs["x"].shape
    args.append(nc.dram_tensor("out_0", shape, F32, kind="ExternalOutput").ap())
    yoco_trunk(nc, *args)
    r = run_bass_kernel_spmd(nc, [arrays], core_ids=[0])
    return r.results[0]["out_0"]
```

```python
import math
from contextlib import ExitStack

import concourse.bass as bass
import numpy as np
from concourse import mybir

F32 = mybir.dt.float32
F32R = mybir.dt.float32r
I32 = mybir.dt.int32
ALU = mybir.AluOpType
ACT = mybir.ActivationFunctionType
AX = mybir.AxisListType

P = 128
RING = 3
CHUNK = 2048
MASKED = -1e30
SUM_EPS = 1e-5
ROPE_THETA = 500000.0
TWO_PI = 2.0 * math.pi
ROUND = 1.5 * 2.0 ** 23


def two_pi_pieces():
    rest, pieces = TWO_PI, []
    for _ in range(3):
        e = math.floor(math.log2(rest)) - 11
        piece = math.floor(rest / 2.0 ** e) * 2.0 ** e
        pieces.append(piece)
        rest -= piece
    return pieces


STEPS = {
    "proj": ("PE", 0.65),
    "drain": ("ACT", 1.0),
    "rope": ("DVE", 1.6),
    "qkT": ("PE", 0.3),
    "qkT_out": ("ACT", 0.55),
    "scores": ("PE", 0.8),
    "mask": ("DVE", 0.7),
    "exp": ("ACT", 0.95),
    "norm": ("DVE", 0.7),
    "probT": ("PE", 0.25),
    "probT_out": ("ACT", 0.45),
    "pv": ("PE", 0.7),
    "square": ("ACT", 0.7),
    "mean": ("DVE", 0.15),
    "subln": ("DVE", 0.5),
    "outT": ("PE", 0.2),
    "out_hi": ("ACT", 0.3),
    "out_lo": ("DVE", 0.4),
    "wo": ("PE", 1.3),
    "split_hi": ("ACT", 0.96),
    "split_lo": ("DVE", 1.15),
}
TURN_FILLS = ("qkT", "probT", "outT")
HOP = 0.12
PATIENCE = {"split_hi": 4.0, "split_lo": 4.0, "drain": 1.0, "rope": 2.0}


def mixer_schedule(layer, first_chunk):
    A = layer == 0
    after = {}

    def add(step, *needs):
        after[step] = [n for n in needs if n in after]

    chunk = lambda cg, kt: first_chunk + 2 * cg + kt // 4
    products = [("proj", 0, kt, 0) for kt in range(8)] + [("proj", 1, kt, 0) for kt in range(4)]
    products += [("proj", 0, kt, 1) for kt in range(8)] + [("proj", 1, kt, 1) for kt in range(4)]
    products += [("proj", cg, kt, st) for cg in range(1, 6) for kt in range(4 if cg == 1 else 0, 8) for st in range(2)]
    products += [("wo", kt, st) for kt in range(4) for st in range(2)]
    products += [("wo", kt, st) for st in range(2) for kt in range(4, 8)]

    previous = None
    uses = {}
    for step in products:
        c = chunk(*step[1:3]) if step[0] == "proj" else first_chunk + 12 + step[1] // 2
        uses[c] = step
    pair = lambda m: m // 2 if A else m
    for c in range(first_chunk + RING, first_chunk + 17):
        for half in range(2):
            after[("split_hi", c, half)], after[("split_lo", c, half)] = [], [("split_hi", c, 1)]
    for step in products:
        c = chunk(*step[1:3]) if step[0] == "proj" else first_chunk + 12 + step[1] // 2
        add(step, ("split_lo", c, 1))
        if previous:
            after[step].append(previous)
        previous = step
    for c in range(first_chunk + RING, first_chunk + 17):
        after[("split_hi", c, 0)].append(uses[c - RING])
    for cg in range(6):
        after[("drain", cg)] = [("proj", cg, 7, 1)]
        if cg + 2 < 6:
            after[("proj", cg + 2, 0, 0)].append(("drain", cg))
        if cg % 3 < 2:
            after[("rope", cg)] = [("drain", cg)]
            for f in range(2):
                after[("qkT", cg, f)] = [("rope", cg)]
                after[("qkT_out", cg, f)] = [("qkT", cg, f)]
            if cg >= 3:
                after[("drain", cg)].append(("qkT", cg - 3, 1))
    after[("wo", 0, 0)].append(("drain", 5))
    for m in range(16):
        g, f = m // 8, m // 4 % 2
        after[("scores", m)] = [("qkT_out", 3 * g, f), ("qkT_out", 3 * g + 1, f)]
        add(("mask", m), ("scores", m), ("exp", m - 2))
        if m >= 2:
            after[("scores", m)].append(("mask", m - 2))
        add(("exp", m), ("mask", m), ("probT", m - 4 if A else m // 2 - 2))
        k = m if A else m // 2
        if A or m % 2:
            add(("norm", k), ("exp", m), ("mean", k - 4))
            add(("probT", k), ("norm", k))
            add(("probT_out", k), ("probT", k), ("pv", k - 2))
            add(("pv", k), ("probT_out", k), ("drain", 3 * g + 2), ("out_lo", pair(k) - 1) if A else ("subln", k - 1))
            if not A:
                add(("square", k), ("pv", k))
                add(("mean", k), ("square", k))
                add(("subln", k), ("mean", k), ("outT", k - 1))
                add(("outT", k), ("subln", k))
            if not A or m % 2:
                add(("out_hi", pair(k)), ("pv", k) if A else ("outT", k))
                add(("out_lo", pair(k)), ("out_hi", pair(k)))
    for kt in range(8):
        for st in range(2):
            after[("wo", kt, st)].append(("out_lo", kt))
    kinds = {}
    for step in after:
        kinds.setdefault(step[0], []).append(step)
    for kind, steps in kinds.items():
        if kind not in ("proj", "wo"):
            steps.sort()

    order = {"PE": [], "ACT": [], "DVE": []}
    free = dict.fromkeys(order, 0.0)
    end = {}
    turn_bank_free = 0.0
    products_left = list(products)
    waiting = {k: list(v) for k, v in kinds.items() if k not in ("proj", "wo")}

    def ready(step):
        times = [0.0]
        for n in after[step]:
            if n not in end:
                return None
            times.append(end[n] + (0.0 if STEPS[n[0]][0] == STEPS[step[0]][0] else HOP))
            if step[0] == "subln" and n[0] == "mean":
                times[-1] += 0.9
        if step[0] in TURN_FILLS:
            if turn_bank_free is None:
                return None
            times.append(turn_bank_free + HOP)
        return max(times)

    while products_left or any(waiting.values()):
        best = None
        for kind, steps in waiting.items():
            if steps and (r := ready(steps[0])) is not None:
                engine = STEPS[kind][0]
                start = max(r, free[engine])
                key = (start, engine == "PE" and -1.0, r + PATIENCE.get(kind, 0.0))
                if best is None or key < best[0]:
                    best = (key, steps[0], start)
        if products_left and (r := ready(products_left[0])) is not None:
            start = max(r, free["PE"])
            key = (start, 1.0, r)
            if best is None or key < best[0]:
                best = (key, products_left[0], start)
        _, step, start = best
        engine, takes = STEPS[step[0]]
        if step[0] == "norm" and not A:
            takes = 1.1
        (products_left if step[0] in ("proj", "wo") else waiting[step[0]]).pop(0)
        free[engine] = end[step] = start + takes
        order[engine].append(step)
        if step[0] in TURN_FILLS:
            turn_bank_free = None
        elif step[0] in ("qkT_out", "probT_out") or not A and step[0] == "out_lo":
            turn_bank_free = end[step]
    return order


def yoco_trunk(nc, x, positions, a_w_qkv, a_w_o, w_kv_shared, b_w_q, b_w_o, b_lambda, b_subln_g,
               ln_g, ln_b, ffn_w_in, ffn_conv_w, ffn_conv_b, ffn_w_out, out):
    SEQ, D = x.shape[1], x.shape[2]
    LAYERS = ln_g.shape[0]
    DFF = ffn_w_out.shape[1]
    ST, KT = SEQ // P, D // P
    FT = DFF // P
    GROUPS = FT // 2
    HALF = D // 2
    ALPHA = (2 * LAYERS) ** 0.25
    SCALE = 64 ** -0.5
    LAMBDA_INIT = 0.8 - 0.6 * math.exp(-0.3 * (LAYERS // 2))
    ROT = 8
    assert (SEQ, D, LAYERS, FT % 2) == (256, 1024, 2, 0)
    QKV_CHUNKS, WO_CHUNKS = 12, 4
    LAYER_CHUNKS = QKV_CHUNKS + WO_CHUNKS + 3 * GROUPS
    CHUNKS = LAYERS * LAYER_CHUNKS
    MAPS = 16

    schedule = [mixer_schedule(layer, layer * LAYER_CHUNKS) for layer in range(LAYERS)]
    fills = [(layer,) + step for layer in range(LAYERS) for step in schedule[layer]["PE"]
             if step[0] in TURN_FILLS]
    fill_of = {fill: n for n, fill in enumerate(fills)}

    def ffn_chunk(layer, i, which):
        base = layer * LAYER_CHUNKS + QKV_CHUNKS + WO_CHUNKS
        if which == 2:
            return base + 3 * i + 2 if isinstance(i, int) and i == GROUPS - 1 else base + 3 * i + 4
        return base + 3 * i - 1 + which if not isinstance(i, int) or i > 0 else base + which

    with ExitStack() as ctx:
        def sb(name, shape, dt=F32):
            return ctx.enter_context(nc.sbuf_tensor(name, shape, dt))

        def sem(name):
            return ctx.enter_context(nc.semaphore(name))

        raw = [sb(f"raw{s}", [P, CHUNK]) for s in range(RING)]
        w_hi = [sb(f"w_hi{s}", [P, CHUNK], F32R) for s in range(RING)]
        w_lo = [sb(f"w_lo{s}", [P, CHUNK], F32R) for s in range(RING)]
        xs = sb("xs", [P, ST, D])
        xT_hi = sb("xT_hi", [P, KT, SEQ], F32R)
        xT_lo = sb("xT_lo", [P, KT, SEQ], F32R)
        rows = [sb("q_rows", [P, ST, HALF]), sb("k_rows", [P, ST, HALF])]
        headT = [sb("qT", [P, KT, SEQ]), sb("kT", [P, KT, SEQ])]
        v_rows = sb("v_rows", [P, ST, D])
        oT_hi = sb("oT_hi", [P, KT, SEQ], F32R)
        oT_lo = sb("oT_lo", [P, KT, SEQ], F32R)
        masked = sb("masked", [P, 2, 3 * P])
        probs = sb("probs", [P, 4, 3 * P])
        probsT = sb("probsT", [P, 2, 3 * P])
        neg_max = sb("neg_max", [P, 4, ST])
        sums = sb("sums", [P, 4, ST])
        recips = sb("recips", [P, 4, ST])
        head_out = sb("head_out", [P, ST, P])
        squares = sb("squares", [P, ST, P])
        mean_sq = sb("mean_sq", [P, 2, ST])
        rms_inv = sb("rms_inv", [P, 2, ST])
        conv = sb("conv", [P, 2, SEQ])
        gelu = sb("gelu", [P, 2, SEQ])
        hidden = sb("hidden", [P, 2, SEQ])
        hT_hi = [sb(f"hT_hi{b}", [P, 2, SEQ], F32R) for b in range(2)]
        hT_lo = [sb(f"hT_lo{b}", [P, 2, SEQ], F32R) for b in range(2)]
        gain = sb("gain", [P, 2, D])
        shift = sb("shift", [P, 2, D])
        conv_rows = sb("conv_rows", [4 * FT, LAYERS, P])
        conv_cols = sb("conv_cols", [P, LAYERS, 4 * FT])
        stats = sb("stats", [P, ST, 2, 6])
        moments = sb("moments", [P, ST, 2])
        var_eps = sb("var_eps", [P, ST])
        std_inv = sb("std_inv", [P, ST])
        minus_half = sb("minus_half", [P, ST])
        ident = sb("ident", [P, P])
        causal = sb("causal", [P, 3 * P])
        zeros = sb("zeros", [P, 4 * P], F32R)
        pos_i = sb("pos_i", [P, ST], I32)
        pos_f = sb("pos_f", [P, ST])
        freq = sb("freq", [P, ROT])
        angle = sb("angle", [P, ST, ROT])
        turns = sb("turns", [P, ST, ROT])
        small = sb("small", [P, ST, ROT])
        sines = sb("sines", [P, 2, ST, ROT])
        cos2 = sb("cos2", [P, ST, 2 * ROT])
        sin2 = sb("sin2", [P, ST, 2 * ROT])
        rot_a = sb("rot_a", [P, ST, KT, 2 * ROT])
        rot_b = sb("rot_b", [P, ST, KT, 2 * ROT])
        lam_in = sb("lam_in", [P, 4, 64])
        lam_prod = sb("lam_prod", [P, 2, 64])
        lam_dot = sb("lam_dot", [P, 2])
        lam_exp = sb("lam_exp", [P, 2])
        neg_lam = sb("neg_lam", [P, 1])
        neg_lam_r = sb("neg_lam_r", [P, 2, ST])
        eps_sq = sb("eps_sq", [P, 4, ST])
        sub_g = sb("sub_g", [P, 1])
        sub_gain = sb("sub_gain", [P, 1])

        def bank(name):
            return ctx.enter_context(nc.psum_tensor(name, [P, 512], F32))

        wide = [bank(f"wide{b}") for b in range(4)]
        score_bank = [bank("score0"), bank("score1")]
        turn_bank = bank("turn")
        out_bank = bank("outb")
        side = [score_bank[0], score_bank[1], turn_bank, out_bank]
        up_bank, gate_bank = side[0:2], side[2:4]

        raw_in = [sem(f"raw_in{s}") for s in range(RING)]
        hi_done, lo_done, chunk_used = sem("hi_done"), sem("lo_done"), sem("chunk_used")
        x_in = [sem(f"x_in{st}") for st in range(ST)]
        small_in, norm_in, out_stored = sem("small_in"), sem("norm_in"), sem("out_stored")
        consts_done, tables_done = sem("consts_done"), sem("tables_done")
        angle_done, sines_done, lam_dot_done, lam_exp_done = (
            sem("angle_done"), sem("sines_done"), sem("lam_dot_done"), sem("lam_exp_done"))
        pool_step, act_step, dve_step = sem("pool_step"), sem("act_step"), sem("dve_step")
        xT_filled, xhi_done, xlo_done = sem("xT_filled"), sem("xhi_done"), sem("xlo_done")
        cols_filled, cols_drained = sem("cols_filled"), sem("cols_drained")
        proj_drained, rope_done = sem("proj_drained"), sem("rope_done")
        turn_filled, turn_drained = sem("turn_filled"), sem("turn_drained")
        scores_done, max_done, exp_done, norm_done = (
            sem("scores_done"), sem("max_done"), sem("exp_done"), sem("norm_done"))
        pv_done, squares_done, eps_done, mean_sq_done, rms_done, head_done = (
            sem("pv_done"), sem("squares_done"), sem("eps_done"), sem("mean_sq_done"), sem("rms_done"), sem("head_done"))
        ohi_done, olo_done = sem("ohi_done"), sem("olo_done")
        y0_done, var_done, std_done, norm_x_done = sem("y0_done"), sem("var_done"), sem("std_done"), sem("norm_x_done")
        up0_done, gate0_done = sem("up0_done"), sem("gate0_done")
        tap_done, conv_done, gelu_done, hidden_done = sem("tap_done"), sem("conv_done"), sem("gelu_done"), sem("hidden_done")
        hhi_done, hlo_done = sem("hhi_done"), sem("hlo_done")

        block = ctx.enter_context(nc.Block())

        @block.sync
        def _(sp):
            def load_x(st):
                sp.dma_start(xs[:, st, :], x[0, st * P:(st + 1) * P, :]).then_inc(x_in[st], 16)

            load_x(0)

            def load(c, slot, dst, src):
                if not isinstance(c, int) or c >= RING:
                    sp.wait_ge(lo_done, c - RING + 1)
                sp.dma_start(dst(raw[slot][:, :]), src).then_inc(raw_in[slot], 16)

            for layer in range(LAYERS):
                base = layer * LAYER_CHUNKS
                for cg in range(6):
                    g, mat = divmod(cg, 3)
                    if layer == 0:
                        w, col = a_w_qkv[0], mat * D + g * HALF
                    else:
                        w, col = (b_w_q[0], g * HALF) if mat == 0 else (w_kv_shared, (mat - 1) * D + g * HALF)
                    for h in range(2):
                        c = base + 2 * cg + h
                        load(c, c % RING, lambda r: r.rearrange("p (k n) -> p k n", k=4),
                             w[4 * P * h:4 * P * (h + 1), col:col + HALF].rearrange("(k p) n -> p k n", p=P))
                        if c == 0:
                            load_x(1)
                wo = (a_w_o if layer == 0 else b_w_o)[0]
                for t in range(WO_CHUNKS):
                    c = base + QKV_CHUNKS + t
                    load(c, c % RING, lambda r: r.rearrange("p (k n) -> p k n", k=2),
                         wo[2 * P * t:2 * P * (t + 1), :].rearrange("(k p) n -> p k n", p=P))

                w_in = ffn_w_in[layer].rearrange("(k p) n -> p k n", p=P)
                w_out = ffn_w_out[layer].rearrange("(k p) n -> p k n", p=P)

                def load_in(i, which):
                    load(ffn_chunk(layer, i, which), ffn_chunk(layer, 1 if not isinstance(i, int) else i, which) % RING,
                         lambda r: r.rearrange("p (k n) -> p k n", k=KT),
                         w_in[:, :, bass.ds(which * DFF + i * 2 * P, 2 * P)])

                def load_out(i):
                    load(ffn_chunk(layer, i, 2), ffn_chunk(layer, 0 if not isinstance(i, int) else i, 2) % RING,
                         lambda r: r.rearrange("p (k n) -> p k n", k=2), w_out[:, bass.ds(2 * i, 2), :])

                load_in(0, 0)
                load_in(0, 1)
                with sp.Fori(1, GROUPS) as i:
                    load_in(i, 0)
                    load_in(i, 1)
                    load_out(i - 1)
                load_out(GROUPS - 1)
            for st in range(ST):
                for half in range(2):
                    cols = slice(half * HALF, (half + 1) * HALF)
                    sp.wait_ge(norm_x_done, 4 * (2 * LAYERS - 1) + 2 * st + half + 1)
                    sp.dma_start(out[0, st * P:(st + 1) * P, cols], xs[:, st, cols]).then_inc(out_stored, 16)
            sp.wait_ge(out_stored, 16 * 2 * ST)

        @block.gpsimd
        def _(pool):
            nc.gpsimd.memset(ident[:, :], 0.0).then_inc(pool_step, 1)
            pool.wait_ge(pool_step, 1)
            nc.gpsimd.affine_select(ident[:, :], ident[:, :], pattern=[[-1, P]], compare_op=ALU.not_equal,
                                    fill=1.0, base=0, channel_multiplier=1).then_inc(consts_done, 1)
            for st in range(ST):
                pool.dma_start(pos_i[:, st:st + 1], positions[0, st * P:(st + 1) * P].rearrange("(p o) -> p o", o=1)
                               ).then_inc(small_in, 16)
            pool.dma_start(lam_in[:, :, :], bass.AP(tensor=b_lambda.tensor, offset=b_lambda.offset, ap=[[0, P], [64, 4], [1, 64]])
                           ).then_inc(small_in, 16)
            pool.dma_start(sub_g[:, :], b_subln_g[0].rearrange("(p o) -> p o", o=1)).then_inc(small_in, 16)
            for layer in range(LAYERS):
                pool.dma_start(conv_rows[0:3 * FT, layer, :],
                               ffn_conv_w[layer].rearrange("t (j p) -> (t j) p", p=P)).then_inc(small_in, 16)
                pool.dma_start(conv_rows[3 * FT:4 * FT, layer, :],
                               ffn_conv_b[layer].rearrange("(j p) -> j p", p=P)).then_inc(small_in, 16)
            for r in range(ROT):
                inv = 1.0 / np.float32(ROPE_THETA) ** np.float32(r * 2.0 / (2 * ROT))
                nc.gpsimd.memset(freq[:, r:r + 1], float(np.float32(inv))).then_inc(consts_done, 1)
            nc.gpsimd.memset(minus_half[:, :], -0.5)
            nc.gpsimd.memset(zeros[:, :].bitcast(F32), 0.0)
            nc.gpsimd.memset(causal[:, :], 0.0).then_inc(pool_step, 1)
            pool.wait_ge(pool_step, 2)
            for b in (0, 2):
                nc.gpsimd.affine_select(causal[:, b * P:(b + 1) * P], causal[:, b * P:(b + 1) * P],
                                        pattern=[[-1, P]], compare_op=ALU.is_ge, fill=MASKED, base=0,
                                        channel_multiplier=1).then_inc(consts_done, 1)
            pool.wait_ge(lo_done, RING)
            for n in range(2 * LAYERS):
                if n % 2 == 0:
                    if n:
                        pool.wait_ge(norm_x_done, 4 * n)
                    for tile, src in ((gain, ln_g), (shift, ln_b)):
                        pool.dma_start(tile[:, :, :], bass.AP(tensor=src.tensor, offset=src.offset + n * D,
                                                              ap=[[0, P], [D, 2], [1, D]])).then_inc(norm_in, 16)
                if n == 2:
                    for p in range(MAPS // 2):
                        pool.wait_ge(mean_sq_done, p + 1)
                        nc.gpsimd.tensor_tensor(rms_inv[:, p % 2, :], mean_sq[:, p % 2, :], minus_half[:, :],
                                                ALU.pow).then_inc(rms_done, 1)
                for st in range(ST):
                    pool.wait_ge(var_done, ST * n + st + 1)
                    nc.gpsimd.tensor_tensor(std_inv[:, st:st + 1], var_eps[:, st:st + 1], minus_half[:, 0:1],
                                            ALU.pow).then_inc(std_done, 1)

        @block.scalar
        def _(act):
            def split_hi(c, slot, round_of, parts=(slice(0, CHUNK),), last=True):
                act.wait_ge(raw_in[slot], round_of)
                if not isinstance(c, int) or c >= RING:
                    act.wait_ge(chunk_used, c - RING + 1)
                for part in parts:
                    ins = nc.scalar.activation(w_hi[slot][:, part], raw[slot][:, part], ACT.Copy)
                if last:
                    ins.then_inc(hi_done, 1)

            def split_static(c, half=None):
                part = slice(0, CHUNK) if half is None else slice(half * CHUNK // 2, (half + 1) * CHUNK // 2)
                if c < CHUNKS:
                    split_hi(c, c % RING, 16 * (c // RING + 1), (part,), half != 0)

            def xT_hi_part(n, fills=range(4)):
                for f in fills:
                    act.wait_ge(xT_filled, 4 * n + f + 1)
                    st, half = divmod(f, 2)
                    nc.scalar.activation(xT_hi[:, 4 * half:4 * half + 4, st * P:(st + 1) * P],
                                         side[f][:, :].rearrange("p (k q) -> p k q", k=4),
                                         ACT.Copy).then_inc(xhi_done, 1)

            xT_hi_part(0, (0, 1))
            split_static(0)
            xT_hi_part(0, (2, 3))
            split_static(1)
            split_static(2)
            act.wait_ge(angle_done, 1)
            nc.scalar.activation(sines[:, 0], angle[:, :, :], ACT.Sin)
            nc.scalar.activation(sines[:, 1], angle[:, :, :], ACT.Sin, scale=0.5).then_inc(sines_done, 1)
            act.wait_ge(lam_dot_done, 1)
            nc.scalar.activation(lam_exp[:, :], lam_dot[:, :], ACT.Exp).then_inc(lam_exp_done, 1)
            for layer in range(LAYERS):
                base = layer * LAYER_CHUNKS
                for kind, m, *rest in schedule[layer]["ACT"]:
                    if kind == "split_hi":
                        split_static(m, rest[0])
                    elif kind == "drain":
                        g, mat = divmod(m, 3)
                        act.wait_ge(chunk_used, base + 2 * m + 2)
                        if mat < 2 and (layer, g) != (0, 0):
                            before = (layer, "qkT", m - 3, 1) if g else (layer - 1, "qkT", m + 3, 1)
                            act.wait_ge(turn_filled, fill_of[before] + 1)
                        for st in range(ST):
                            dst = rows[mat][:, st, :] if mat < 2 else v_rows[:, st, g * HALF:(g + 1) * HALF]
                            nc.scalar.activation(dst, wide[2 * (m % 2) + st][:, :], ACT.Copy).then_inc(proj_drained, 1)
                    elif kind == "qkT_out":
                        (g, mat), f = divmod(m, 3), rest[0]
                        act.wait_ge(turn_filled, fill_of[(layer, "qkT", m, f)] + 1)
                        nc.scalar.activation(headT[mat][:, 4 * g + 2 * f:4 * g + 2 * f + 2, :],
                                             turn_bank[:, :].rearrange("p (k q) -> p k q", k=2),
                                             ACT.Copy).then_inc(turn_drained, 1)
                    elif kind == "exp":
                        if layer == 0 and m == 0:
                            act.wait_ge(cols_filled, 1)
                            for n in range(LAYERS):
                                last = nc.scalar.activation(conv_cols[:, n, :], out_bank[:, 4 * FT * n:4 * FT * (n + 1)],
                                                            ACT.Copy)
                            last.then_inc(cols_drained, 1)
                        act.wait_ge(max_done, MAPS * layer + m + 1)
                        if layer == 0 and m >= 4:
                            act.wait_ge(turn_filled, fill_of[(0, "probT", m - 4)] + 1)
                        elif layer == 1:
                            before = (1, "probT", m // 2 - 2) if m >= 4 else (0, "probT", MAPS - 4 + m)
                            act.wait_ge(turn_filled, fill_of[before] + 1)
                        for q, (lo, hi) in enumerate(((0, P), (P, 3 * P))):
                            last = nc.scalar.activation(probs[:, m % 4, lo:hi], masked[:, m % 2, lo:hi], ACT.Exp,
                                                        scale=-1.0, bias=neg_max[:, m % 4, q:q + 1],
                                                        accum_out=sums[:, m % 4, q:q + 1])
                        last.then_inc(exp_done, 1)
                    elif kind == "probT_out":
                        act.wait_ge(turn_filled, fill_of[(layer, "probT", m)] + 1)
                        if layer == 0 and m >= 2:
                            act.wait_ge(pv_done, m - 1)
                        elif layer == 1:
                            act.wait_ge(pv_done, MAPS + m - 1)
                        nc.scalar.activation(probsT[:, m % 2, :], turn_bank[:, 0:3 * P], ACT.Copy).then_inc(turn_drained, 1)
                    elif kind == "square":
                        act.wait_ge(pv_done, MAPS + m + 1)
                        if m >= 2:
                            act.wait_ge(head_done, m - 1)
                        for st in range(ST):
                            last = nc.scalar.activation(squares[:, st, :], out_bank[:, st * P:(st + 1) * P], ACT.Square,
                                                        accum_out=mean_sq[:, m % 2, st:st + 1])
                        last.then_inc(squares_done, 1)
                    elif kind == "out_hi" and layer == 0:
                        act.wait_ge(pv_done, 2 * m + 2)
                        nc.scalar.activation(oT_hi[:, m, :], out_bank[:, 0:SEQ], ACT.Copy).then_inc(ohi_done, 1)
                    elif kind == "out_hi":
                        act.wait_ge(turn_filled, fill_of[(1, "outT", m)] + 1)
                        nc.scalar.activation(oT_hi[:, m, :], turn_bank[:, 0:SEQ], ACT.Copy,
                                             scale=sub_gain[:, 0:1]).then_inc(ohi_done, 1)
                xT_hi_part(2 * layer + 1)
                split_static(base + QKV_CHUNKS + WO_CHUNKS + 1)
                split_static(base + QKV_CHUNKS + WO_CHUNKS + 2)

                def ffn_group(i, peeled):
                    t = GROUPS * layer + i
                    cu, cg = ffn_chunk(layer, i, 0), ffn_chunk(layer, i, 1)
                    at = 1 if peeled == "loop" else i
                    slot_u, slot_g = ffn_chunk(layer, at, 0) % RING, ffn_chunk(layer, at, 1) % RING

                    def split_after(c, slot):
                        if peeled == "loop":
                            first = ffn_chunk(layer, 1, 0) + {slot_u: 0, slot_g: 1}.get(slot, 2) + RING
                            split_hi(c + RING, slot, 16 * (first // RING + 1) + 16 * (i - 1))
                        else:
                            split_static(c + RING)

                    for tt in range(2):
                        if tt == 0:
                            act.wait_ge(up0_done, t + 1)
                        else:
                            act.wait_ge(chunk_used, cu + 1)
                        nc.scalar.activation(conv[:, tt, :], up_bank[tt][:, 0:SEQ], ACT.Identity,
                                             scale=conv_cols[:, layer, bass.ds(2 * FT + 2 * i + tt, 1)],
                                             bias=conv_cols[:, layer, bass.ds(3 * FT + 2 * i + tt, 1)]
                                             ).then_inc(tap_done, 1)
                    for tt in range(2):
                        act.wait_ge(conv_done, 2 * t + tt + 1)
                        if peeled == "loop" or t > 0:
                            act.wait_ge(hidden_done, 2 * t + tt - 1)
                        nc.scalar.activation(gelu[:, tt, :], conv[:, tt, :], ACT.Gelu_apprx_tanh).then_inc(gelu_done, 1)
                    split_after(cu, slot_u)
                    if peeled != "last":
                        split_after(cg, slot_g)
                    into = hT_hi[1 if peeled == "last" else 0]
                    for tt in range(2):
                        act.wait_ge(hidden_done, 2 * t + tt + 1)
                        if tt == 0 and peeled == "loop":
                            act.wait_ge(chunk_used, cg + 2)
                        nc.scalar.activation(into[:, tt, :], hidden[:, tt, :], ACT.Copy).then_inc(hhi_done, 1)
                    if peeled == "last":
                        split_after(cg, slot_g)
                    if peeled == "loop":
                        split_after(cg + 1, (slot_g + 1) % RING)

                ffn_group(0, "first")
                with act.Fori(1, GROUPS - 1) as i:
                    ffn_group(i, "loop")
                ffn_group(GROUPS - 1, "last")
                if layer + 1 < LAYERS:
                    xT_hi_part(2 * layer + 2, (0, 1))
                    split_static(base + LAYER_CHUNKS + 1)
                    split_static(base + LAYER_CHUNKS + 2)
                    xT_hi_part(2 * layer + 2, (2, 3))

        @block.vector
        def _(dve):
            steps = {"n": 0, "i": None, "from": 0, "per": 0}

            def link(ins):
                steps["n"] += 1
                ins.then_inc(dve_step, 1)
                if steps["i"] is None:
                    dve.wait_ge(dve_step, steps["n"])
                else:
                    dve.wait_ge(dve_step, steps["n"] + (steps["i"] - 1) * steps["per"])

            def split_lo(c, slot, part=slice(0, CHUNK), last=True):
                dve.wait_ge(hi_done, c + 1)
                ins = nc.vector.tensor_tensor(w_lo[slot][:, part], raw[slot][:, part], w_hi[slot][:, part].bitcast(F32),
                                              ALU.subtract)
                if last:
                    ins.then_inc(lo_done, 1)

            def split_static(c, half=None):
                part = slice(0, CHUNK) if half is None else slice(half * CHUNK // 2, (half + 1) * CHUNK // 2)
                if c < CHUNKS:
                    split_lo(c, c % RING, part, half != 0)

            def xT_lo_part(n, fills):
                for f in fills:
                    dve.wait_ge(xhi_done, 4 * n + f + 1)
                    st, half = divmod(f, 2)
                    part = (slice(None), slice(4 * half, 4 * half + 4), slice(st * P, (st + 1) * P))
                    nc.vector.tensor_tensor(xT_lo[part], side[f][:, :].rearrange("p (k q) -> p k q", k=4),
                                            xT_hi[part].bitcast(F32), ALU.subtract).then_inc(xlo_done, 1)

            def residual(n, st):
                if st == 0:
                    dve.wait_ge(y0_done, n + 1)
                else:
                    dve.wait_ge(chunk_used, (n // 2) * LAYER_CHUNKS + (QKV_CHUNKS + WO_CHUNKS if n % 2 == 0
                                                                       else LAYER_CHUNKS))
                for half in range(2):
                    part = xs[:, st, half * HALF:(half + 1) * HALF]
                    last = nc.vector.scalar_tensor_tensor(part, part, ALPHA, wide[2 * st + half][:, :],
                                                          ALU.mult, ALU.add)
                link(last)

            def layer_norm(n, st):
                for half in range(2):
                    last = nc.vector.bn_stats(stats[:, st, half, :], xs[:, st, half * HALF:(half + 1) * HALF])
                link(last)
                link(nc.vector.bn_aggr(moments[:, st, :], stats[:, st, :, :].rearrange("p a b -> p (a b)")))
                nc.vector.tensor_scalar(var_eps[:, st:st + 1], moments[:, st, 1:2], SUM_EPS, None,
                                        ALU.add).then_inc(var_done, 1)
                if st == 0:
                    dve.wait_ge(norm_in, 32 * (n // 2 + 1))
                for half in range(2):
                    cols = slice(half * HALF, (half + 1) * HALF)
                    last = nc.vector.scalar_tensor_tensor(xs[:, st, cols], xs[:, st, cols], moments[:, st, 0:1],
                                                          gain[:, n % 2, cols], ALU.subtract, ALU.mult)
                link(last)
                dve.wait_ge(std_done, ST * n + st + 1)
                for half in range(2):
                    cols = slice(half * HALF, (half + 1) * HALF)
                    nc.vector.scalar_tensor_tensor(xs[:, st, cols], xs[:, st, cols], std_inv[:, st:st + 1],
                                                   shift[:, n % 2, cols], ALU.mult, ALU.add).then_inc(norm_x_done, 1)

            xT_lo_part(0, (0, 1))
            split_static(0)
            xT_lo_part(0, (2, 3))
            split_static(1)
            split_static(2)

            dve.wait_ge(small_in, 16 * 8)
            dve.wait_ge(consts_done, 1 + ROT)
            link(nc.vector.tensor_copy(pos_f[:, :], pos_i[:, :]))
            for st in range(ST):
                last = nc.vector.tensor_scalar(angle[:, st, :], freq[:, :], pos_f[:, st:st + 1], None, ALU.mult)
            link(last)
            pieces = two_pi_pieces()
            link(nc.vector.memset(small[:, :, :], 0.0))
            for times in (4096.0, 1.0):
                link(nc.vector.tensor_scalar(turns[:, :, :], angle[:, :, :], 1.0 / (TWO_PI * times), None, ALU.mult))
                link(nc.vector.tensor_scalar(turns[:, :, :], turns[:, :, :], ROUND, None, ALU.add))
                link(nc.vector.tensor_scalar(turns[:, :, :], turns[:, :, :], ROUND, None, ALU.subtract))
                for n, piece in enumerate(pieces):
                    into = angle if n < 2 else small
                    link(nc.vector.scalar_tensor_tensor(into[:, :, :], turns[:, :, :], -piece * times,
                                                        into[:, :, :], ALU.mult, ALU.add))
            link(nc.vector.tensor_tensor(angle[:, :, :], angle[:, :, :], small[:, :, :], ALU.add))
            link(nc.vector.tensor_scalar(turns[:, :, :], angle[:, :, :], 1.0 / TWO_PI, None, ALU.mult))
            link(nc.vector.tensor_scalar(turns[:, :, :], turns[:, :, :], ROUND, None, ALU.add))
            link(nc.vector.tensor_scalar(turns[:, :, :], turns[:, :, :], ROUND, None, ALU.subtract))
            for piece in (pieces[0], TWO_PI - pieces[0]):
                link(nc.vector.scalar_tensor_tensor(angle[:, :, :], turns[:, :, :], -piece, angle[:, :, :],
                                                    ALU.mult, ALU.add))
            nc.vector.tensor_scalar(angle[:, :, :], angle[:, :, :], 3.1415925, -3.1415925, ALU.min,
                                    ALU.max).then_inc(angle_done, 1)
            link(nc.vector.tensor_tensor(lam_prod[:, :, :], lam_in[:, :, :].rearrange("p (a b) d -> p a b d", b=2)[:, :, 0, :],
                                         lam_in[:, :, :].rearrange("p (a b) d -> p a b d", b=2)[:, :, 1, :], ALU.mult))
            nc.vector.tensor_reduce(lam_dot[:, :], lam_prod[:, :, :], AX.X, ALU.add).then_inc(lam_dot_done, 1)
            nc.vector.tensor_scalar(sub_gain[:, :], sub_g[:, :], 1.0 - LAMBDA_INIT, None, ALU.mult)
            dve.wait_ge(sines_done, 1)
            link(nc.vector.tensor_tensor(small[:, :, :], sines[:, 1], sines[:, 1], ALU.mult))
            for h in range(2):
                nc.vector.tensor_scalar(cos2[:, :, h * ROT:(h + 1) * ROT], small[:, :, :], -2.0, 1.0, ALU.mult, ALU.add)
                last = nc.vector.tensor_scalar(sin2[:, :, h * ROT:(h + 1) * ROT], sines[:, 0], 2.0 * h - 1.0, None,
                                               ALU.mult)
            link(last)
            dve.wait_ge(lam_exp_done, 1)
            link(nc.vector.tensor_tensor(neg_lam[:, :], lam_exp[:, 1:2], lam_exp[:, 0:1], ALU.subtract))
            link(nc.vector.tensor_scalar(neg_lam[:, :], neg_lam[:, :], LAMBDA_INIT, None, ALU.subtract))
            dve.wait_ge(consts_done, 3 + ROT)

            for layer in range(LAYERS):
                base = layer * LAYER_CHUNKS
                for kind, m, *rest in schedule[layer]["DVE"]:
                    if kind == "split_lo":
                        split_static(m, rest[0])
                    elif kind == "rope":
                        dve.wait_ge(proj_drained, 12 * layer + 2 * m + 2)
                        for st in range(ST):
                            heads = rows[m % 3][:, st, :].rearrange("p (h d) -> p h d", d=64)

                            def over_heads(table, a, b):
                                return table[:, st, a:b].unsqueeze(1).broadcast_to([P, KT, b - a])

                            nc.vector.tensor_tensor(rot_a[:, st], heads[:, :, 0:2 * ROT],
                                                    over_heads(cos2, 0, 2 * ROT), ALU.mult)
                            nc.vector.tensor_tensor(rot_b[:, st, :, 0:ROT], heads[:, :, ROT:2 * ROT],
                                                    over_heads(sin2, 0, ROT), ALU.mult)
                            last = nc.vector.tensor_tensor(rot_b[:, st, :, ROT:2 * ROT], heads[:, :, 0:ROT],
                                                           over_heads(sin2, ROT, 2 * ROT), ALU.mult)
                        link(last)
                        for st in range(ST):
                            heads = rows[m % 3][:, st, :].rearrange("p (h d) -> p h d", d=64)
                            last = nc.vector.tensor_tensor(heads[:, :, 0:2 * ROT], rot_a[:, st], rot_b[:, st], ALU.add)
                        last.then_inc(rope_done, 1)
                    elif kind == "mask":
                        j = MAPS * layer + m
                        dve.wait_ge(scores_done, j + 1)
                        if j >= 2:
                            dve.wait_ge(exp_done, j - 1)
                        for q, (lo, hi) in enumerate(((0, P), (P, 3 * P))):
                            last = nc.vector.tensor_tensor_reduce(
                                out=masked[:, m % 2, lo:hi], in0=score_bank[m % 2][:, lo:hi], in1=causal[:, lo:hi],
                                scale=-SCALE, scalar=3e38, op0=ALU.add, op1=ALU.min,
                                accum_out=neg_max[:, m % 4, q:q + 1])
                        last.then_inc(max_done, 1)
                    elif kind == "norm" and layer == 0:
                        dve.wait_ge(exp_done, m + 1)
                        link(nc.vector.reciprocal(recips[:, m % 4, :], sums[:, m % 4, :]))
                        for q, (lo, hi) in enumerate(((0, P), (P, 3 * P))):
                            last = nc.vector.tensor_scalar(probs[:, m % 4, lo:hi], probs[:, m % 4, lo:hi],
                                                           recips[:, m % 4, q:q + 1], None, ALU.mult)
                        last.then_inc(norm_done, 1)
                    elif kind == "norm":
                        a = 2 * (m % 2)
                        dve.wait_ge(exp_done, MAPS + 2 * m + 2)
                        link(nc.vector.reciprocal(recips[:, a, :], sums[:, a + 1, :]))
                        link(nc.vector.scalar_tensor_tensor(neg_lam_r[:, m % 2, :], sums[:, a, :], neg_lam[:, 0:1],
                                                            recips[:, a, :], ALU.mult, ALU.mult))
                        for q, (lo, hi) in enumerate(((0, P), (P, 3 * P))):
                            last = nc.vector.scalar_tensor_tensor(probs[:, a, lo:hi], probs[:, a + 1, lo:hi],
                                                                  neg_lam_r[:, m % 2, q:q + 1], probs[:, a, lo:hi],
                                                                  ALU.mult, ALU.add)
                        last.then_inc(norm_done, 1)
                        nc.vector.scalar_tensor_tensor(eps_sq[:, m % 4, :], sums[:, a, :], SUM_EPS, sums[:, a, :],
                                                       ALU.mult, ALU.mult).then_inc(eps_done, 1)
                    elif kind == "mean":
                        dve.wait_ge(squares_done, m + 1)
                        dve.wait_ge(eps_done, m + 1)
                        nc.vector.scalar_tensor_tensor(mean_sq[:, m % 2, :], mean_sq[:, m % 2, :], 1.0 / P,
                                                       eps_sq[:, m % 4, :], ALU.mult, ALU.add).then_inc(mean_sq_done, 1)
                    elif kind == "subln":
                        dve.wait_ge(rms_done, m + 1)
                        if m >= 1:
                            dve.wait_ge(turn_filled, fill_of[(1, "outT", m - 1)] + 1)
                        for st in range(ST):
                            last = nc.vector.tensor_scalar(head_out[:, st, :], out_bank[:, st * P:(st + 1) * P],
                                                           rms_inv[:, m % 2, st:st + 1], None, ALU.mult)
                        last.then_inc(head_done, 1)
                    elif kind == "out_lo":
                        dve.wait_ge(ohi_done, 8 * layer + m + 1)
                        if layer == 0:
                            nc.vector.tensor_tensor(oT_lo[:, m, :], out_bank[:, 0:SEQ], oT_hi[:, m, :].bitcast(F32),
                                                    ALU.subtract).then_inc(olo_done, 1)
                        else:
                            nc.vector.scalar_tensor_tensor(oT_lo[:, m, :], turn_bank[:, 0:SEQ], sub_gain[:, 0:1],
                                                           oT_hi[:, m, :].bitcast(F32), ALU.mult,
                                                           ALU.subtract).then_inc(turn_drained, 1)
                residual(2 * layer, 0)
                layer_norm(2 * layer, 0)
                residual(2 * layer, 1)
                xT_lo_part(2 * layer + 1, (0, 1))
                layer_norm(2 * layer, 1)
                xT_lo_part(2 * layer + 1, (2, 3))
                split_static(base + QKV_CHUNKS + WO_CHUNKS + 1)
                split_static(base + QKV_CHUNKS + WO_CHUNKS + 2)

                def ffn_group(i, peeled):
                    t = GROUPS * layer + i
                    cu, cg = ffn_chunk(layer, i, 0), ffn_chunk(layer, i, 1)
                    at = 1 if peeled == "loop" else i
                    slot_u, slot_g = ffn_chunk(layer, at, 0) % RING, ffn_chunk(layer, at, 1) % RING

                    def split_after(c, slot):
                        if peeled == "loop":
                            split_lo(c + RING, slot)
                        else:
                            split_static(c + RING)

                    for tt in range(2):
                        dve.wait_ge(tap_done, 2 * t + tt + 1)
                        link(nc.vector.scalar_tensor_tensor(conv[:, tt, 1:SEQ], up_bank[tt][:, 0:SEQ - 1],
                                                            conv_cols[:, layer, bass.ds(FT + 2 * i + tt, 1)],
                                                            conv[:, tt, 1:SEQ], ALU.mult, ALU.add))
                        nc.vector.scalar_tensor_tensor(conv[:, tt, 2:SEQ], up_bank[tt][:, 0:SEQ - 2],
                                                       conv_cols[:, layer, bass.ds(2 * i + tt, 1)],
                                                       conv[:, tt, 2:SEQ], ALU.mult, ALU.add).then_inc(conv_done, 1)
                    split_after(cu, slot_u)
                    for tt in range(2):
                        dve.wait_ge(gelu_done, 2 * t + tt + 1)
                        if tt == 0:
                            dve.wait_ge(gate0_done, t + 1)
                        else:
                            dve.wait_ge(chunk_used, cg + 1)
                        if peeled == "loop" or t > 0:
                            dve.wait_ge(hhi_done, 2 * t + tt - 1)
                        nc.vector.tensor_tensor(hidden[:, tt, :], gelu[:, tt, :], gate_bank[tt][:, 0:SEQ],
                                                ALU.mult).then_inc(hidden_done, 1)
                    if peeled != "last":
                        split_after(cg, slot_g)
                    b = 1 if peeled == "last" else 0
                    for tt in range(2):
                        dve.wait_ge(hhi_done, 2 * t + tt + 1)
                        nc.vector.tensor_tensor(hT_lo[b][:, tt, :], hidden[:, tt, :], hT_hi[b][:, tt, :].bitcast(F32),
                                                ALU.subtract).then_inc(hlo_done, 1)
                    if peeled == "last":
                        split_after(cg, slot_g)
                    if peeled == "loop":
                        split_after(cg + 1, (slot_g + 1) % RING)

                ffn_group(0, "first")
                before = steps["n"]
                LINKS = 2
                with dve.Fori(1, GROUPS - 1) as i:
                    steps["i"], steps["per"] = i, LINKS
                    ffn_group(i, "loop")
                assert steps["n"] == before + LINKS
                steps["n"], steps["i"] = before + LINKS * (GROUPS - 2), None
                ffn_group(GROUPS - 1, "last")
                residual(2 * layer + 1, 0)
                layer_norm(2 * layer + 1, 0)
                if layer + 1 < LAYERS:
                    xT_lo_part(2 * layer + 2, (0, 1))
                    split_static(base + LAYER_CHUNKS + 1)
                residual(2 * layer + 1, 1)
                if layer + 1 < LAYERS:
                    split_static(base + LAYER_CHUNKS + 2)
                layer_norm(2 * layer + 1, 1)
                if layer + 1 < LAYERS:
                    xT_lo_part(2 * layer + 2, (2, 3))

        @block.tensor
        def _(pe):
            def product(dst, a_hi, a_lo, b_hi, b_lo, start, stop):
                nc.tensor.matmul(dst, a_hi, b_hi, start=start, stop=False, skip_group_check=True)
                nc.tensor.matmul(dst, a_hi, b_lo, start=False, stop=False, skip_group_check=True)
                return nc.tensor.matmul(dst, a_lo, b_hi, start=False, stop=stop, skip_group_check=True)

            def x_transposes(n, fills=range(4)):
                for f in fills:
                    st, half = divmod(f, 2)
                    if n == 0:
                        pe.wait_ge(x_in[st], 16)
                        pe.wait_ge(consts_done, 1)
                    else:
                        pe.wait_ge(norm_x_done, 4 * (n - 1) + f + 1)
                    for k in range(4):
                        last = nc.tensor.transpose(side[f][:, k * P:(k + 1) * P],
                                                   xs[:, st, (4 * half + k) * P:(4 * half + k + 1) * P], ident[:, :])
                    last.then_inc(xT_filled, 1)

            x_transposes(0)
            for layer in range(LAYERS):
                base = layer * LAYER_CHUNKS
                for kind, m, *rest in schedule[layer]["PE"]:
                    j = MAPS * layer + m
                    if kind == "proj":
                        cg, (kt, st) = m, rest
                        c = base + 2 * cg + kt // 4
                        if cg == 0 and kt % 4 == 0:
                            if layer and kt == 0:
                                x_transposes(2 * layer, (2 * st, 2 * st + 1))
                            pe.wait_ge(xlo_done, 8 * layer + 2 * st + kt // 4 + 1)
                        if kt % 4 == 0:
                            pe.wait_ge(lo_done, c + 1)
                        if kt == 0 and st == 0 and cg >= 2:
                            pe.wait_ge(proj_drained, 12 * layer + 2 * cg - 2)
                        cols = slice((kt % 4) * HALF, (kt % 4 + 1) * HALF)
                        rs = slice(st * P, (st + 1) * P)
                        last = product(wide[2 * (cg % 2) + st][:, :], xT_hi[:, kt, rs], xT_lo[:, kt, rs],
                                       w_hi[c % RING][:, cols], w_lo[c % RING][:, cols], kt == 0, kt == KT - 1)
                        if kt % 4 == 3 and st == 1:
                            last.then_inc(chunk_used, 1)
                    elif kind == "qkT":
                        cg, f = m, rest[0]
                        n = fill_of[(layer, "qkT", cg, f)]
                        g, mat = divmod(cg, 3)
                        if f == 0:
                            pe.wait_ge(rope_done, 4 * layer + 2 * g + mat + 1)
                        if n:
                            pe.wait_ge(turn_drained, n)
                        for k in range(2):
                            for st in range(ST):
                                last = nc.tensor.transpose(turn_bank[:, (2 * k + st) * P:(2 * k + st + 1) * P],
                                                           rows[mat][:, st, (2 * f + k) * P:(2 * f + k + 1) * P],
                                                           ident[:, :])
                        last.then_inc(turn_filled, 1)
                    elif kind == "scores":
                        half = slice(64 * (m % 2), 64 * (m % 2) + 64)
                        qT, kT = headT[0][half, m // 2, :], headT[1][half, m // 2, :]
                        if m % 4 == 0:
                            g, f = m // 8, m // 4 % 2
                            for cg in (3 * g, 3 * g + 1):
                                pe.wait_ge(turn_drained, fill_of[(layer, "qkT", cg, f)] + 1)
                        if layer == 0 and m == 0:
                            pe.wait_ge(small_in, 16 * 8)
                            for n in range(LAYERS):
                                last = nc.tensor.transpose(out_bank[:, 4 * FT * n:4 * FT * (n + 1)], conv_rows[:, n, :],
                                                           ident[0:4 * FT, 0:4 * FT])
                            last.then_inc(cols_filled, 1)
                        if j >= 2:
                            pe.wait_ge(max_done, j - 1)
                        bank_ = score_bank[m % 2]
                        nc.tensor.matmul(bank_[:, 0:P], qT[:, 0:P], kT[:, 0:P], start=True, stop=True)
                        nc.tensor.matmul(bank_[:, P:3 * P], qT[:, P:2 * P], kT[:, :], start=True,
                                         stop=True).then_inc(scores_done, 1)
                    elif kind == "probT":
                        n = fill_of[(layer, "probT", m)]
                        slot = m % 4 if layer == 0 else 2 * (m % 2)
                        pe.wait_ge(norm_done, (0 if layer == 0 else MAPS) + m + 1)
                        pe.wait_ge(turn_drained, n)
                        for b in range(3):
                            last = nc.tensor.transpose(turn_bank[:, b * P:(b + 1) * P], probs[:, slot, b * P:(b + 1) * P],
                                                       ident[:, :])
                        last.then_inc(turn_filled, 1)
                    elif kind == "pv":
                        pe.wait_ge(turn_drained, fill_of[(layer, "probT", m)] + 1)
                        if layer == 0 and m % 8 == 0 or layer == 1 and m % 4 == 0:
                            g = m // 8 if layer == 0 else m // 4
                            pe.wait_ge(proj_drained, 12 * layer + 6 * g + 6)
                        pT = probsT[:, m % 2, :]
                        if layer == 0:
                            if m == 0:
                                pe.wait_ge(cols_drained, 1)
                            if m % 2 == 0 and m >= 2:
                                pe.wait_ge(olo_done, m // 2)
                            part = out_bank[64 * (m % 2):64 * (m % 2) + 64, :]
                            nc.tensor.matmul(part[:, 0:SEQ], v_rows[:, 0, 64 * m:64 * m + 64], pT[:, 0:SEQ], start=True,
                                             stop=False)
                            nc.tensor.matmul(part[:, P:SEQ], v_rows[:, 1, 64 * m:64 * m + 64], pT[:, SEQ:3 * P],
                                             start=False, stop=True).then_inc(pv_done, 1)
                        else:
                            if m == 0:
                                pe.wait_ge(olo_done, 8)
                            else:
                                pe.wait_ge(head_done, m)
                            v = [v_rows[:, st, P * m:P * (m + 1)] for st in range(ST)]
                            nc.tensor.matmul(out_bank[:, 0:P], pT[:, 0:P], v[0], start=True, stop=True)
                            nc.tensor.matmul(out_bank[:, P:SEQ], pT[:, P:SEQ], v[0], start=True, stop=False)
                            nc.tensor.matmul(out_bank[:, P:SEQ], pT[:, SEQ:3 * P], v[1], start=False,
                                             stop=True).then_inc(pv_done, 1)
                    elif kind == "outT":
                        pe.wait_ge(head_done, m + 1)
                        pe.wait_ge(turn_drained, fill_of[(1, "outT", m)])
                        for st in range(ST):
                            last = nc.tensor.transpose(turn_bank[:, st * P:(st + 1) * P], head_out[:, st, :], ident[:, :])
                        last.then_inc(turn_filled, 1)
                    elif kind == "wo":
                        kt, st = m, rest[0]
                        c = base + QKV_CHUNKS + kt // 2
                        if st == 0:
                            if layer == 0:
                                pe.wait_ge(olo_done, kt + 1)
                            else:
                                pe.wait_ge(turn_drained, fill_of[(1, "outT", kt)] + 1)
                            if kt % 2 == 0:
                                pe.wait_ge(lo_done, c + 1)
                            if kt == 0:
                                pe.wait_ge(proj_drained, 12 * layer + 12)
                        rs = slice(st * P, (st + 1) * P)
                        for half in range(2):
                            cols = slice((2 * (kt % 2) + half) * HALF, (2 * (kt % 2) + half + 1) * HALF)
                            last = product(wide[2 * st + half][:, :], oT_hi[:, kt, rs], oT_lo[:, kt, rs],
                                           w_hi[c % RING][:, cols], w_lo[c % RING][:, cols], kt == 0, kt == KT - 1)
                        if st == 1 and kt % 2 == 1:
                            last.then_inc(chunk_used, 1)
                        elif kt == KT - 1:
                            last.then_inc(y0_done, 1)

                x_transposes(2 * layer + 1)
                for b in range(4):
                    nc.tensor.matmul(wide[b][:, :], zeros[:, 0:P], zeros[:, :], start=True, stop=True)
                pe.wait_ge(xlo_done, 8 * layer + 8)

                def features(banks, slot, free, done0):
                    for tt in range(2):
                        if free is not None:
                            pe.wait_ge(*free[tt])
                        for kt in range(KT):
                            cols = slice(kt * 2 * P + tt * P, kt * 2 * P + (tt + 1) * P)
                            last = product(banks[tt][:, 0:SEQ], w_hi[slot][:, cols], w_lo[slot][:, cols],
                                           xT_hi[:, kt, :], xT_lo[:, kt, :], kt == 0, kt == KT - 1)
                        last.then_inc(done0 if tt == 0 else chunk_used, 1)

                def second_product(i, slot, sts, final=False):
                    if 0 in sts:
                        pe.wait_ge(lo_done, ffn_chunk(layer, i, 2) + 1)
                        pe.wait_ge(hlo_done, 2 * (GROUPS * layer + i) + 2)
                    b = 1 if final else 0
                    for st in sts:
                        rs = slice(st * P, (st + 1) * P)
                        for tt in range(2):
                            for half in range(2):
                                cols = slice((2 * tt + half) * HALF, (2 * tt + half + 1) * HALF)
                                last = product(wide[2 * st + half][:, :], hT_hi[b][:, tt, rs], hT_lo[b][:, tt, rs],
                                               w_hi[slot][:, cols], w_lo[slot][:, cols], False, final and tt == 1)
                        if st == 1:
                            last.then_inc(chunk_used, 1)
                        elif final:
                            last.then_inc(y0_done, 1)

                def ffn_group(i, peeled):
                    t = GROUPS * layer + i
                    at = 1 if peeled == "loop" else i
                    first = peeled == "first"
                    pe.wait_ge(lo_done, ffn_chunk(layer, i, 0) + 1)
                    features(up_bank, ffn_chunk(layer, at, 0) % RING,
                             None if first else [(conv_done, 2 * t - 1), (conv_done, 2 * t)], up0_done)
                    pe.wait_ge(lo_done, ffn_chunk(layer, i, 1) + 1)
                    features(gate_bank, ffn_chunk(layer, at, 1) % RING,
                             None if first else [(hidden_done, 2 * t - 1), (hidden_done, 2 * t)], gate0_done)
                    if peeled == "loop":
                        second_product(i - 1, (ffn_chunk(layer, at, 1) + 1) % RING, range(ST))

                ffn_group(0, "first")
                with pe.Fori(1, GROUPS - 1) as i:
                    ffn_group(i, "loop")
                ffn_group(GROUPS - 1, "last")
                for st in range(ST):
                    for i in (GROUPS - 2, GROUPS - 1):
                        second_product(i, ffn_chunk(layer, i, 2) % RING, (st,), i == GROUPS - 1)


_INS = ["x", "positions", "a_w_qkv", "a_w_o", "w_kv_shared", "b_w_q", "b_w_o", "b_lambda", "b_subln_g", "ln_g",
        "ln_b", "ffn_w_in", "ffn_conv_w", "ffn_conv_b", "ffn_w_out"]


def kernel(**inputs):
    from concourse import bacc
    from concourse.bass_utils import run_bass_kernel_spmd

    nc = bacc.Bacc("TRN2", target_bir_lowering=False, num_devices=1)
    arrays, args = {}, []
    for name in _INS:
        a = np.ascontiguousarray(inputs[name])
        arrays[f"in_{name}"] = a
        args.append(nc.dram_tensor(f"in_{name}", a.shape, mybir.dt.from_np(a.dtype), kind="ExternalInput").ap())
    shape = inputs["x"].shape
    args.append(nc.dram_tensor("out_0", shape, F32, kind="ExternalOutput").ap())
    yoco_trunk(nc, *args)
    r = run_bass_kernel_spmd(nc, [arrays], core_ids=[0])
    return r.results[0]["out_0"]
```

```python
import math
from contextlib import ExitStack

import concourse.bass as bass
import numpy as np
from concourse import mybir

F32 = mybir.dt.float32
F32R = mybir.dt.float32r
I32 = mybir.dt.int32
ALU = mybir.AluOpType
ACT = mybir.ActivationFunctionType
AX = mybir.AxisListType

P = 128
RING = 3
CHUNK = 2048
FIRST = 3
PIECES = 4
WARM_UP = (6, 5)
MASKED = -1e30
SUM_EPS = 1e-5
ROPE_THETA = 500000.0
TWO_PI = 2.0 * math.pi
ROUND = 1.5 * 2.0 ** 23


def two_pi_pieces():
    rest, pieces = TWO_PI, []
    for _ in range(3):
        e = math.floor(math.log2(rest)) - 11
        piece = math.floor(rest / 2.0 ** e) * 2.0 ** e
        pieces.append(piece)
        rest -= piece
    return pieces


STEPS = {
    "proj": ("PE", 0.65),
    "drain": ("ACT", 0.96),
    "rope": ("DVE", 1.7),
    "qkT": ("PE", 0.43),
    "qkT_out": ("ACT", 0.48),
    "scores": ("PE", 0.64),
    "mask": ("DVE", 0.6),
    "exp": ("ACT", 0.88),
    "norm": ("DVE", 0.7),
    "probT": ("PE", 0.33),
    "probT_out": ("ACT", 0.37),
    "pv": ("PE", 0.64),
    "pv_out": ("ACT", 0.31),
    "square": ("ACT", 0.5),
    "mean": ("DVE", 0.07),
    "subln": ("DVE", 0.4),
    "outT": ("PE", 0.22),
    "out_hi": ("ACT", 0.3),
    "out_lo": ("DVE", 0.37),
    "wo": ("PE", 0.65),
    "split_hi": ("ACT", 0.95),
    "split_lo": ("DVE", 1.14),
}
TURN_FILLS = ("qkT", "probT", "outT")
HOP = 0.2
PATIENCE = {"split_hi": 7.0, "split_lo": 5.0, "drain": 1.0, "rope": 2.0, "out_hi": -1.5, "out_lo": -1.0}


def mixer_schedule(layer, first_chunk):
    A = layer == 0
    after = {}

    def add(step, *needs):
        after[step] = [n for n in needs if n in after]

    chunk = lambda cg, kt: first_chunk + 2 * cg + kt // 4
    ahead = [] if A else [("proj", 1, kt, 0) for kt in range(4)]
    products = [("proj", 0, kt, 0) for kt in range(8)] + ahead + [("proj", 0, kt, 1) for kt in range(8)]
    products += [("proj", 1, kt, st) for kt in range(4) for st in range(2) if ("proj", 1, kt, st) not in ahead]
    products += [("proj", cg, kt, st) for cg in range(1, 6) for kt in range(4 if cg == 1 else 0, 8) for st in range(2)]
    products += [("wo", kt, st, half) for kt in range(4) for st in range(2) for half in range(2)]
    products += [("wo", kt, 0, half) for half in range(2) for kt in range(4, 8)]
    products += [("wo", kt, 1, half) for kt in range(4, 6) for half in range(2)]
    products += [("wo", kt, 1, half) for half in range(2) for kt in range(6, 8)]

    previous = None
    uses = {}
    for step in products:
        c = chunk(*step[1:3]) if step[0] == "proj" else first_chunk + 12 + step[1] // 2
        uses[c] = step
    pair = lambda m: m // 2 if A else m
    for c in range(first_chunk + RING, first_chunk + 17):
        for half in range(2):
            after[("split_hi", c, half)], after[("split_lo", c, half)] = [], [("split_hi", c, 1)]
    for step in products:
        c = chunk(*step[1:3]) if step[0] == "proj" else first_chunk + 12 + step[1] // 2
        add(step, ("split_lo", c, 1))
        if previous:
            after[step].append(previous)
        previous = step
    for c in range(first_chunk + RING, first_chunk + 17):
        after[("split_hi", c, 0)].append(uses[c - RING])
    for cg in range(6):
        after[("drain", cg)] = [("proj", cg, 7, 1)]
        if cg + 2 < 6:
            after[("proj", cg + 2, 0, 0)].append(("drain", cg))
        if cg % 3 < 2:
            after[("rope", cg)] = [("drain", cg)]
            for f in range(2):
                after[("qkT", cg, f)] = [("rope", cg)]
                after[("qkT_out", cg, f)] = [("qkT", cg, f)]
            if cg >= 3:
                after[("drain", cg)].append(("qkT", cg - 3, 1))
    after[("wo", 0, 0, 0)].append(("drain", 4))
    after[("wo", 0, 1, 0)].append(("drain", 5))
    for m in range(16):
        g, f = m // 8, m // 4 % 2
        after[("scores", m)] = [("qkT_out", 3 * g, f), ("qkT_out", 3 * g + 1, f)]
        add(("mask", m), ("scores", m), ("exp", m - 2))
        if m >= 2:
            after[("scores", m)].append(("mask", m - 2))
        add(("exp", m), ("mask", m), ("probT", m - 4 if A else m // 2 - 2))
        k = m if A else m // 2
        if A or m % 2:
            add(("norm", k), ("exp", m), ("mean", k - 4))
            add(("probT", k), ("norm", k))
            add(("probT_out", k), ("probT", k), ("pv", k - 2))
            add(("pv", k), ("probT_out", k), ("drain", 3 * g + 2), ("out_lo", pair(k) - 1) if A else ("pv_out", k - 1))
            if not A:
                add(("pv_out", k), ("pv", k), ("subln", k - 2))
                add(("square", k), ("pv_out", k))
                add(("mean", k), ("square", k))
                add(("subln", k), ("mean", k), ("outT", k - 1))
                add(("outT", k), ("subln", k))
            if not A or m % 2:
                add(("out_hi", pair(k)), ("pv", k) if A else ("outT", k))
                add(("out_lo", pair(k)), ("out_hi", pair(k)))
    for kt in range(8):
        for st in range(2):
            for half in range(2):
                after[("wo", kt, st, half)].append(("out_lo", kt))
    kinds = {}
    for step in after:
        kinds.setdefault(step[0], []).append(step)
    for kind, steps in kinds.items():
        if kind not in ("proj", "wo"):
            steps.sort()

    order = {"PE": [], "ACT": [], "DVE": []}
    free = dict.fromkeys(order, 0.0)
    if A:
        free["DVE"] = free["ACT"] = 12.0
    end = {}
    turn_bank_free = 0.0
    products_left = list(products)
    waiting = {k: list(v) for k, v in kinds.items() if k not in ("proj", "wo")}

    def ready(step):
        times = [0.0]
        for n in after[step]:
            if n not in end:
                return None
            times.append(end[n] + (0.0 if STEPS[n[0]][0] == STEPS[step[0]][0] else HOP))
            if step[0] == "subln" and n[0] == "mean":
                times[-1] += 0.9
        if step[0] in TURN_FILLS:
            if turn_bank_free is None:
                return None
            times.append(turn_bank_free + HOP)
        return max(times)

    while products_left or any(waiting.values()):
        best = None
        for kind, steps in waiting.items():
            if steps and (r := ready(steps[0])) is not None:
                engine = STEPS[kind][0]
                start = max(r, free[engine])
                key = (start, engine == "PE" and -1.0, r + PATIENCE.get(kind, 0.0))
                if best is None or key < best[0]:
                    best = (key, steps[0], start)
        if products_left and (r := ready(products_left[0])) is not None:
            start = max(r, free["PE"])
            key = (start, 1.0, r)
            if best is None or key < best[0]:
                best = (key, products_left[0], start)
        _, step, start = best
        engine, takes = STEPS[step[0]]
        if step[0] == "norm" and not A:
            takes = 1.1
        (products_left if step[0] in ("proj", "wo") else waiting[step[0]]).pop(0)
        free[engine] = end[step] = start + takes
        order[engine].append(step)
        if step[0] in TURN_FILLS:
            turn_bank_free = None
        elif step[0] in ("qkT_out", "probT_out") or not A and step[0] == "out_lo":
            turn_bank_free = end[step]
    return order


def yoco_trunk(nc, x, positions, a_w_qkv, a_w_o, w_kv_shared, b_w_q, b_w_o, b_lambda, b_subln_g,
               ln_g, ln_b, ffn_w_in, ffn_conv_w, ffn_conv_b, ffn_w_out, out):
    SEQ, D = x.shape[1], x.shape[2]
    LAYERS = ln_g.shape[0]
    DFF = ffn_w_out.shape[1]
    ST, KT = SEQ // P, D // P
    FT = DFF // P
    GROUPS = FT // 2
    HALF = D // 2
    ALPHA = (2 * LAYERS) ** 0.25
    SCALE = 64 ** -0.5
    LAMBDA_INIT = 0.8 - 0.6 * math.exp(-0.3 * (LAYERS // 2))
    ROT = 8
    assert (SEQ, D, LAYERS, FT % 2) == (256, 1024, 2, 0)
    QKV_CHUNKS, WO_CHUNKS = 12, 4
    LAYER_CHUNKS = QKV_CHUNKS + WO_CHUNKS + 3 * GROUPS
    CHUNKS = LAYERS * LAYER_CHUNKS
    MAPS = 16
    POOL_SPLITS = {}
    for layer in range(LAYERS):
        c = layer * LAYER_CHUNKS + QKV_CHUNKS + WO_CHUNKS
        for st in range(ST):
            POOL_SPLITS[2 * layer, st] = ([(c + st, 0), (c + st, 1)], [])
        c = (layer + 1) * LAYER_CHUNKS
        if layer + 1 < LAYERS:
            for st in range(ST):
                POOL_SPLITS[2 * layer + 1, st] = ([(c + 2 * st, 0)], [(c + 2 * st, 1)])
    POOL_CHUNKS = sorted({c for parts in POOL_SPLITS.values() for c, _ in parts[0]})

    def pool_count(c, half):
        return 2 * POOL_CHUNKS.index(c) + half + 1

    schedule = [mixer_schedule(layer, layer * LAYER_CHUNKS) for layer in range(LAYERS)]
    fills = [(layer,) + step for layer in range(LAYERS) for step in schedule[layer]["PE"]
             if step[0] in TURN_FILLS]
    fill_of = {fill: n for n, fill in enumerate(fills)}

    def ffn_chunk(layer, i, which):
        base = layer * LAYER_CHUNKS + QKV_CHUNKS + WO_CHUNKS
        if which == 2:
            return base + 3 * i + 2 if isinstance(i, int) and i == GROUPS - 1 else base + 3 * i + 4
        return base + 3 * i - 1 + which if not isinstance(i, int) or i > 0 else base + which

    def up_of(first, tt):
        return wide[2 + tt][:, 0:SEQ] if first else up_bank[tt][:, 0:SEQ]

    def gate_of(first, tt):
        return wide[2 + tt][:, SEQ:2 * SEQ] if first else gate_bank[tt][:, 0:SEQ]

    with ExitStack() as ctx:
        def sb(name, shape, dt=F32):
            return ctx.enter_context(nc.sbuf_tensor(name, shape, dt))

        def sem(name):
            return ctx.enter_context(nc.semaphore(name))

        raw = [sb(f"raw{s}", [P, CHUNK]) for s in range(RING)]
        w_hi = [sb(f"w_hi{s}", [P, CHUNK], F32R) for s in range(RING)]
        w_lo = [sb(f"w_lo{s}", [P, CHUNK], F32R) for s in range(RING)]
        xs = sb("xs", [P, ST, D])
        xT_hi = sb("xT_hi", [P, KT, SEQ], F32R)
        xT_lo = sb("xT_lo", [P, KT, SEQ], F32R)
        rows = [sb("q_rows", [P, ST, HALF]), sb("k_rows", [P, ST, HALF])]
        token_rows = rows[0]
        headT = [sb("qT", [P, KT, SEQ]), sb("kT", [P, KT, SEQ])]
        v_rows = sb("v_rows", [P, ST, D])
        oT_hi = sb("oT_hi", [P, KT, SEQ], F32R)
        oT_lo = sb("oT_lo", [P, KT, SEQ], F32R)
        masked = sb("masked", [P, 2, 3 * P])
        probs = sb("probs", [P, 4, 3 * P])
        probsT = sb("probsT", [P, 2, 3 * P])
        neg_max = sb("neg_max", [P, 4, ST])
        sums = sb("sums", [P, 4, ST])
        recips = sb("recips", [P, 4, ST])
        head_rows = sb("head_rows", [P, 2, SEQ])
        head_out = sb("head_out", [P, ST, P])
        squares = sb("squares", [P, ST, P])
        mean_sq = sb("mean_sq", [P, 2, ST])
        rms_inv = sb("rms_inv", [P, 2, ST])
        conv = sb("conv", [P, 2, SEQ])
        gelu = sb("gelu", [P, 2, SEQ])
        hidden = sb("hidden", [P, 2, SEQ])
        hT_hi = [sb(f"hT_hi{b}", [P, 2, SEQ], F32R) for b in range(2)]
        hT_lo = [sb(f"hT_lo{b}", [P, 2, SEQ], F32R) for b in range(2)]
        gain = sb("gain", [P, 2, D])
        shift = sb("shift", [P, 2, D])
        conv_rows = sb("conv_rows", [4 * FT, LAYERS, P])
        conv_cols = sb("conv_cols", [P, LAYERS, 4 * FT])
        stats = sb("stats", [P, ST, 2, 6])
        moments = sb("moments", [P, ST, 2])
        var_eps = sb("var_eps", [P, ST])
        std_inv = sb("std_inv", [P, ST])
        minus_half = sb("minus_half", [P, ST])
        ident = sb("ident", [P, P])
        causal = sb("causal", [P, 3 * P])
        zeros = sb("zeros", [P, 4 * P], F32R)
        pos_i = sb("pos_i", [P, ST], I32)
        pos_f = sb("pos_f", [P, ST])
        freq = sb("freq", [P, ROT])
        angle = sb("angle", [P, ST, ROT])
        turns = sb("turns", [P, ST, ROT])
        whole = sb("whole", [P, ST, ROT])
        small = sb("small", [P, ST, ROT])
        sines = sb("sines", [P, 2, ST, ROT])
        cos2 = sb("cos2", [P, ST, 2 * ROT])
        sin2 = sb("sin2", [P, ST, 2 * ROT])
        rot_a = sb("rot_a", [P, ST, KT, 2 * ROT])
        rot_b = sb("rot_b", [P, ST, KT, 2 * ROT])
        lam_in = sb("lam_in", [P, 4, 64])
        lam_prod = sb("lam_prod", [P, 2, 64])
        lam_dot = sb("lam_dot", [P, 2])
        lam_exp = sb("lam_exp", [P, 2])
        neg_lam = sb("neg_lam", [P, 1])
        neg_lam_r = sb("neg_lam_r", [P, 2, ST])
        eps_sq = sb("eps_sq", [P, 4, ST])
        sub_g = sb("sub_g", [P, 1])
        sub_gain = sb("sub_gain", [P, 1])

        def bank(name):
            return ctx.enter_context(nc.psum_tensor(name, [P, 512], F32))

        wide = [bank(f"wide{b}") for b in range(4)]
        score_bank = [bank("score0"), bank("score1")]
        turn_bank = bank("turn")
        out_bank = bank("outb")
        side = [score_bank[0], score_bank[1], turn_bank, out_bank]
        up_bank, gate_bank = side[0:2], side[2:4]

        raw_in = [sem(f"raw_in{s}") for s in range(RING)]
        hi_done, lo_done, chunk_used = sem("hi_done"), sem("lo_done"), sem("chunk_used")
        x_in = [sem(f"x_in{st}") for st in range(ST)]
        pos_in, small_in, norm_in, out_stored = sem("pos_in"), sem("small_in"), sem("norm_in"), sem("out_stored")
        consts_done = sem("consts_done")
        angle_done, sines_done, lam_dot_done, lam_exp_done = (
            sem("angle_done"), sem("sines_done"), sem("lam_dot_done"), sem("lam_exp_done"))
        pool_step, dve_step = sem("pool_step"), sem("dve_step")
        xT_filled, xhi_done, xlo_done = sem("xT_filled"), sem("xhi_done"), sem("xlo_done")
        cols_filled, cols_drained = sem("cols_filled"), sem("cols_drained")
        proj_drained, rope_done = sem("proj_drained"), sem("rope_done")
        turn_filled, turn_drained = sem("turn_filled"), sem("turn_drained")
        scores_done, max_done, exp_done, norm_done = (
            sem("scores_done"), sem("max_done"), sem("exp_done"), sem("norm_done"))
        pv_done, squares_done, eps_done, mean_sq_done, rms_done, head_done = (
            sem("pv_done"), sem("squares_done"), sem("eps_done"), sem("mean_sq_done"), sem("rms_done"), sem("head_done"))
        ohi_done, olo_done = sem("ohi_done"), sem("olo_done")
        y_done, var_done, std_done, norm_x_done = sem("y_done"), sem("var_done"), sem("std_done"), sem("norm_x_done")
        up0_done, gate0_done = sem("up0_done"), sem("gate0_done")
        stats_done, head_rows_done, zeros_done = sem("stats_done"), sem("head_rows_done"), sem("zeros_done")
        gained_done, scaled_done = sem("gained_done"), sem("scaled_done")
        first_in = [sem(f"first_in{c}") for c in range(FIRST)]
        hi_pieces, lo_pieces, pool_lo_done = sem("hi_pieces"), sem("lo_pieces"), sem("pool_lo_done")
        tokens_done, tokens_out, first_done = sem("tokens_done"), sem("tokens_out"), sem("first_done")
        tap_done, conv_done, gelu_done, hidden_done = sem("tap_done"), sem("conv_done"), sem("gelu_done"), sem("hidden_done")
        hhi_done, hlo_done = sem("hhi_done"), sem("hlo_done")

        block = ctx.enter_context(nc.Block())

        @block.sync
        def _(sp):
            def load_x(st):
                sp.dma_start(xs[:, st, :], x[0, st * P:(st + 1) * P, :]).then_inc(x_in[st], 16)

            def load_small():
                sp.dma_start(lam_in[:, :, :], bass.AP(tensor=b_lambda.tensor, offset=b_lambda.offset,
                                                          ap=[[0, P], [64, 4], [1, 64]])
                               ).then_inc(small_in, 16)
                sp.dma_start(sub_g[:, :], b_subln_g[0].rearrange("(p o) -> p o", o=1)).then_inc(small_in, 16)
                for layer in range(LAYERS):
                    sp.dma_start(conv_rows[0:3 * FT, layer, :],
                                   ffn_conv_w[layer].rearrange("t (j p) -> (t j) p", p=P)).then_inc(small_in, 16)
                    sp.dma_start(conv_rows[3 * FT:4 * FT, layer, :],
                                   ffn_conv_b[layer].rearrange("(j p) -> j p", p=P)).then_inc(small_in, 16)

            load_x(0)

            def load(c, slot, dst, src):
                if isinstance(c, int) and c - RING in POOL_CHUNKS:
                    sp.wait_ge(pool_lo_done, pool_count(c - RING, 1))
                elif not isinstance(c, int) or c >= RING:
                    sp.wait_ge(lo_done, c - RING + 1)
                sp.dma_start(dst(raw[slot][:, :]), src).then_inc(raw_in[slot], 16)

            for layer in range(LAYERS):
                base = layer * LAYER_CHUNKS
                for cg in range(6):
                    g, mat = divmod(cg, 3)
                    if layer == 0:
                        w, col = a_w_qkv[0], mat * D + g * HALF
                    else:
                        w, col = (b_w_q[0], g * HALF) if mat == 0 else (w_kv_shared, (mat - 1) * D + g * HALF)
                    for h in range(2):
                        c = base + 2 * cg + h
                        src = w[4 * P * h:4 * P * (h + 1), col:col + HALF].rearrange("(k p) n -> p k n", p=P)
                        if c < FIRST:
                            sp.dma_start(raw[c][:, 0:CHUNK // 2].rearrange("p (k n) -> p k n", k=2),
                                         src[:, 0:2, :]).then_inc(first_in[c], 16)
                            sp.dma_start(raw[c][:, CHUNK // 2:CHUNK].rearrange("p (k n) -> p k n", k=2),
                                         src[:, 2:4, :]).then_inc(raw_in[c], 16)
                        else:
                            load(c, c % RING, lambda r: r.rearrange("p (k n) -> p k n", k=4), src)
                        if c == 1:
                            load_x(1)
                        if c == FIRST - 1:
                            load_small()
                wo = (a_w_o if layer == 0 else b_w_o)[0]
                for t in range(WO_CHUNKS):
                    c = base + QKV_CHUNKS + t
                    load(c, c % RING, lambda r: r.rearrange("p (k n) -> p k n", k=2),
                         wo[2 * P * t:2 * P * (t + 1), :].rearrange("(k p) n -> p k n", p=P))

                w_in = ffn_w_in[layer].rearrange("(k p) n -> p k n", p=P)
                w_out = ffn_w_out[layer].rearrange("(k p) n -> p k n", p=P)

                def load_in(i, which):
                    load(ffn_chunk(layer, i, which), ffn_chunk(layer, 1 if not isinstance(i, int) else i, which) % RING,
                         lambda r: r.rearrange("p (k n) -> p k n", k=KT),
                         w_in[:, :, bass.ds(which * DFF + i * 2 * P, 2 * P)])

                def load_out(i):
                    load(ffn_chunk(layer, i, 2), ffn_chunk(layer, 0 if not isinstance(i, int) else i, 2) % RING,
                         lambda r: r.rearrange("p (k n) -> p k n", k=2), w_out[:, bass.ds(2 * i, 2), :])

                load_in(0, 0)
                load_in(0, 1)

                def load_group(i):
                    load_in(i, 0)
                    load_in(i, 1)
                    load_out(i - 1)

                load_group(1)
                with sp.Fori(2, GROUPS) as i:
                    load_group(i)
                load_out(GROUPS - 1)
            for st in range(ST):
                for half in range(2):
                    cols = slice(half * HALF, (half + 1) * HALF)
                    sp.wait_ge(norm_x_done, 4 * (2 * LAYERS - 1) + 2 * st + half + 1)
                    sp.dma_start(out[0, st * P:(st + 1) * P, cols], xs[:, st, cols]).then_inc(out_stored, 16)
            sp.wait_ge(out_stored, 16 * 2 * ST)

        @block.gpsimd
        def _(pool):
            nc.gpsimd.memset(ident[:, :], 0.0).then_inc(pool_step, 1)
            pool.wait_ge(pool_step, 1)
            nc.gpsimd.affine_select(ident[:, :], ident[:, :], pattern=[[-1, P]], compare_op=ALU.not_equal,
                                    fill=1.0, base=0, channel_multiplier=1).then_inc(consts_done, 1)
            for st in range(ST):
                pool.dma_start(pos_i[:, st:st + 1], positions[0, st * P:(st + 1) * P].rearrange("(p o) -> p o", o=1)
                               ).then_inc(pos_in, 16)
            for r in range(ROT):
                inv = 1.0 / np.float32(ROPE_THETA) ** np.float32(r * 2.0 / (2 * ROT))
                nc.gpsimd.memset(freq[:, r:r + 1], float(np.float32(inv)))
            n_links = [1]

            def pool_link(ins):
                n_links[0] += 1
                ins.then_inc(pool_step, 1)
                pool.wait_ge(pool_step, n_links[0])

            pool.wait_ge(pos_in, 16 * ST)
            pool_link(nc.gpsimd.tensor_copy(pos_f[:, :], pos_i[:, :]))
            for st in range(ST):
                last = nc.gpsimd.tensor_scalar(angle[:, st, :], freq[:, :], pos_f[:, st:st + 1], None, ALU.mult)
            pool_link(last)
            pieces = two_pi_pieces()
            pool_link(nc.gpsimd.memset(small[:, :, :], 0.0))
            for times in (4096.0, 1.0):
                pool_link(nc.gpsimd.tensor_scalar(turns[:, :, :], angle[:, :, :], 1.0 / (TWO_PI * times), None, ALU.mult))
                pool_link(nc.gpsimd.tensor_scalar(turns[:, :, :], turns[:, :, :], ROUND, None, ALU.add))
                pool_link(nc.gpsimd.tensor_scalar(turns[:, :, :], turns[:, :, :], ROUND, None, ALU.subtract))
                for n, piece in enumerate(pieces):
                    into = angle if n < 2 else small
                    pool_link(nc.gpsimd.tensor_scalar(whole[:, :, :], turns[:, :, :], -piece * times, None, ALU.mult))
                    pool_link(nc.gpsimd.tensor_tensor(into[:, :, :], whole[:, :, :], into[:, :, :], ALU.add))
            pool_link(nc.gpsimd.tensor_tensor(angle[:, :, :], angle[:, :, :], small[:, :, :], ALU.add))
            pool_link(nc.gpsimd.tensor_scalar(turns[:, :, :], angle[:, :, :], 1.0 / TWO_PI, None, ALU.mult))
            pool_link(nc.gpsimd.tensor_scalar(turns[:, :, :], turns[:, :, :], ROUND, None, ALU.add))
            pool_link(nc.gpsimd.tensor_scalar(turns[:, :, :], turns[:, :, :], ROUND, None, ALU.subtract))
            for piece in (pieces[0], TWO_PI - pieces[0]):
                pool_link(nc.gpsimd.tensor_scalar(whole[:, :, :], turns[:, :, :], -piece, None, ALU.mult))
                pool_link(nc.gpsimd.tensor_tensor(angle[:, :, :], whole[:, :, :], angle[:, :, :], ALU.add))
            nc.gpsimd.tensor_scalar(angle[:, :, :], angle[:, :, :], 3.1415925, -3.1415925, ALU.min,
                                    ALU.max).then_inc(angle_done, 1)
            nc.gpsimd.memset(minus_half[:, :], -0.5)
            nc.gpsimd.memset(causal[:, :], 0.0).then_inc(pool_step, 1)
            pool.wait_ge(pool_step, n_links[0] + 1)
            for b in (0, 2):
                nc.gpsimd.affine_select(causal[:, b * P:(b + 1) * P], causal[:, b * P:(b + 1) * P],
                                        pattern=[[-1, P]], compare_op=ALU.is_ge, fill=MASKED, base=0,
                                        channel_multiplier=1).then_inc(consts_done, 1)

            def pool_split_lo(c, half):
                pool.wait_ge(hi_done, c + 1)
                part = slice(half * CHUNK // 2, (half + 1) * CHUNK // 2)
                nc.gpsimd.tensor_tensor(w_lo[c % RING][:, part], raw[c % RING][:, part],
                                        w_hi[c % RING][:, part].bitcast(F32), ALU.subtract).then_inc(pool_lo_done, 1)

            pool.wait_ge(lo_done, RING)
            for n in range(2 * LAYERS):
                if n % 2 == 0:
                    if n:
                        pool.wait_ge(norm_x_done, 4 * n)
                    for tile, src in ((gain, ln_g), (shift, ln_b)):
                        pool.dma_start(tile[:, :, :], bass.AP(tensor=src.tensor, offset=src.offset + n * D,
                                                              ap=[[0, P], [D, 2], [1, D]])).then_inc(norm_in, 16)
                if n == 2:
                    for p in range(MAPS // 2):
                        pool.wait_ge(mean_sq_done, p + 1)
                        nc.gpsimd.tensor_tensor(rms_inv[:, p % 2, :], mean_sq[:, p % 2, :], minus_half[:, :],
                                                ALU.pow).then_inc(rms_done, 1)
                for st in range(ST):
                    before, after = POOL_SPLITS.get((n, st), ((), ()))
                    for c, half in before:
                        pool_split_lo(c, half)
                    pool.wait_ge(var_done, ST * n + st + 1)
                    nc.gpsimd.tensor_tensor(std_inv[:, st:st + 1], var_eps[:, st:st + 1], minus_half[:, 0:1],
                                            ALU.pow).then_inc(std_done, 1)
                    if (n, st) == (2 * LAYERS - 1, 0):
                        for half in range(2):
                            cols = slice(half * HALF, (half + 1) * HALF)
                            pool.wait_ge(scaled_done, half + 1)
                            nc.gpsimd.tensor_tensor(xs[:, 0, cols], xs[:, 0, cols], shift[:, n % 2, cols],
                                                    ALU.add).then_inc(norm_x_done, 1)
                    for c, half in after:
                        pool_split_lo(c, half)

        @block.scalar
        def _(act):
            def split_hi(c, slot, round_of, parts=(slice(0, CHUNK),), last=True):
                act.wait_ge(raw_in[slot], round_of)
                if not isinstance(c, int) or c >= RING:
                    act.wait_ge(chunk_used, c - RING + 1)
                for part in parts:
                    ins = nc.scalar.activation(w_hi[slot][:, part], raw[slot][:, part], ACT.Copy)
                if last:
                    ins.then_inc(hi_done, 1)

            def split_static(c, half=None):
                part = slice(0, CHUNK) if half is None else slice(half * CHUNK // 2, (half + 1) * CHUNK // 2)
                if c < CHUNKS:
                    split_hi(c, c % RING, 16 * (c // RING + 1), (part,), half != 0)

            def xT_hi_part(n, fills=range(4)):
                for f in fills:
                    act.wait_ge(xT_filled, 4 * n + f + 1)
                    st, half = divmod(f, 2)
                    nc.scalar.activation(xT_hi[:, 4 * half:4 * half + 4, st * P:(st + 1) * P],
                                         side[f][:, :].rearrange("p (k q) -> p k q", k=4),
                                         ACT.Copy).then_inc(xhi_done, 1)

            def first_piece(c, q):
                act.wait_ge(*((first_in[c], 16) if q < PIECES // 2 else (raw_in[c], 16)))
                part = slice(q * CHUNK // PIECES, (q + 1) * CHUNK // PIECES)
                nc.scalar.activation(w_hi[c][:, part], raw[c][:, part], ACT.Copy).then_inc(
                    hi_pieces if q < PIECES - 1 else hi_done, 1)

            for c in range(FIRST):
                for q in range(PIECES):
                    if c == 0 and q % 2 == 0:
                        xT_hi_part(0, (q // 2,))
                    elif c == 2 and q == 0:
                        xT_hi_part(0, (2, 3))
                    first_piece(c, q)
            act.wait_ge(angle_done, 1)
            nc.scalar.activation(sines[:, 0], angle[:, :, :], ACT.Sin)
            nc.scalar.activation(sines[:, 1], angle[:, :, :], ACT.Sin, scale=0.5).then_inc(sines_done, 1)
            for layer in range(LAYERS):
                base = layer * LAYER_CHUNKS
                for kind, m, *rest in schedule[layer]["ACT"]:
                    if kind == "split_hi":
                        split_static(m, rest[0])
                    elif kind == "drain":
                        g, mat = divmod(m, 3)
                        act.wait_ge(chunk_used, base + 2 * m + 2)
                        if mat < 2 and (layer, g) != (0, 0):
                            before = (layer, "qkT", m - 3, 1) if g else (layer - 1, "qkT", m + 3, 1)
                            act.wait_ge(turn_filled, fill_of[before] + 1)
                        for st in range(ST):
                            dst = rows[mat][:, st, :] if mat < 2 else v_rows[:, st, g * HALF:(g + 1) * HALF]
                            nc.scalar.activation(dst, wide[2 * (m % 2) + st][:, :], ACT.Copy).then_inc(proj_drained, 1)
                    elif kind == "qkT_out":
                        (g, mat), f = divmod(m, 3), rest[0]
                        act.wait_ge(turn_filled, fill_of[(layer, "qkT", m, f)] + 1)
                        nc.scalar.activation(headT[mat][:, 4 * g + 2 * f:4 * g + 2 * f + 2, :],
                                             turn_bank[:, :].rearrange("p (k q) -> p k q", k=2),
                                             ACT.Copy).then_inc(turn_drained, 1)
                    elif kind == "exp":
                        if layer == 0 and m == 0:
                            act.wait_ge(cols_filled, 1)
                            for n in range(LAYERS):
                                last = nc.scalar.activation(conv_cols[:, n, :], out_bank[:, 4 * FT * n:4 * FT * (n + 1)],
                                                            ACT.Copy)
                            last.then_inc(cols_drained, 1)
                        if layer == 1 and m == 0:
                            act.wait_ge(lam_dot_done, 1)
                            nc.scalar.activation(lam_exp[:, :], lam_dot[:, :], ACT.Exp).then_inc(lam_exp_done, 1)
                        act.wait_ge(max_done, MAPS * layer + m + 1)
                        if layer == 0 and m >= 4:
                            act.wait_ge(turn_filled, fill_of[(0, "probT", m - 4)] + 1)
                        elif layer == 1:
                            before = (1, "probT", m // 2 - 2) if m >= 4 else (0, "probT", MAPS - 4 + m)
                            act.wait_ge(turn_filled, fill_of[before] + 1)
                        for q, (lo, hi) in enumerate(((0, P), (P, 3 * P))):
                            last = nc.scalar.activation(probs[:, m % 4, lo:hi], masked[:, m % 2, lo:hi], ACT.Exp,
                                                        scale=-1.0, bias=neg_max[:, m % 4, q:q + 1],
                                                        accum_out=sums[:, m % 4, q:q + 1])
                        last.then_inc(exp_done, 1)
                    elif kind == "probT_out":
                        act.wait_ge(turn_filled, fill_of[(layer, "probT", m)] + 1)
                        if layer == 0 and m >= 2:
                            act.wait_ge(pv_done, m - 1)
                        elif layer == 1:
                            act.wait_ge(pv_done, MAPS + m - 1)
                        nc.scalar.activation(probsT[:, m % 2, :], turn_bank[:, 0:3 * P], ACT.Copy).then_inc(turn_drained, 1)
                    elif kind == "pv_out":
                        act.wait_ge(pv_done, MAPS + m + 1)
                        if m >= 2:
                            act.wait_ge(head_done, m - 1)
                        nc.scalar.activation(head_rows[:, m % 2, :], out_bank[:, 0:SEQ],
                                             ACT.Copy).then_inc(head_rows_done, 1)
                    elif kind == "square":
                        act.wait_ge(head_rows_done, m + 1)
                        for st in range(ST):
                            last = nc.scalar.activation(squares[:, st, :], head_rows[:, m % 2, st * P:(st + 1) * P],
                                                        ACT.Square, accum_out=mean_sq[:, m % 2, st:st + 1])
                        last.then_inc(squares_done, 1)
                    elif kind == "out_hi" and layer == 0:
                        act.wait_ge(pv_done, 2 * m + 2)
                        nc.scalar.activation(oT_hi[:, m, :], out_bank[:, 0:SEQ], ACT.Copy).then_inc(ohi_done, 1)
                    elif kind == "out_hi":
                        act.wait_ge(turn_filled, fill_of[(1, "outT", m)] + 1)
                        nc.scalar.activation(oT_hi[:, m, :], turn_bank[:, 0:SEQ], ACT.Copy,
                                             scale=sub_gain[:, 0:1]).then_inc(ohi_done, 1)
                c = base + QKV_CHUNKS + WO_CHUNKS
                split_static(c + 1)
                xT_hi_part(2 * layer + 1, (0, 1))
                split_static(c + 2)
                xT_hi_part(2 * layer + 1, (2, 3))

                def ffn_group(i, peeled):
                    t = GROUPS * layer + i
                    cu, cg = ffn_chunk(layer, i, 0), ffn_chunk(layer, i, 1)
                    at = 2 if peeled == "loop" else i
                    first = peeled == "first"
                    slot_u, slot_g = ffn_chunk(layer, at, 0) % RING, ffn_chunk(layer, at, 1) % RING

                    def split_after(c, slot):
                        if peeled == "loop":
                            loop_first = ffn_chunk(layer, 2, 0) + {slot_u: 0, slot_g: 1}.get(slot, 2) + RING
                            split_hi(c + RING, slot, 16 * (loop_first // RING + 1) + 16 * (i - 2))
                        else:
                            split_static(c + RING)

                    if first:
                        for st in range(ST):
                            act.wait_ge(*((tokens_done, layer + 1) if st == 0 else (chunk_used, cg + 1)))
                            nc.scalar.activation(token_rows[:, st, :], wide[st][:, :], ACT.Copy).then_inc(tokens_out, 1)
                            split_after((cu, cg)[st], (slot_u, slot_g)[st])
                    for tt in range(2):
                        if first:
                            act.wait_ge(first_done, 2 * layer + tt + 1)
                        elif tt == 0:
                            act.wait_ge(up0_done, t - layer)
                        else:
                            act.wait_ge(chunk_used, cu + 1)
                        nc.scalar.activation(conv[:, tt, :], up_of(first, tt), ACT.Identity,
                                             scale=conv_cols[:, layer, bass.ds(2 * FT + 2 * i + tt, 1)],
                                             bias=conv_cols[:, layer, bass.ds(3 * FT + 2 * i + tt, 1)]
                                             ).then_inc(tap_done, 1)
                    if peeled == "last":
                        split_static(cu + RING, 0)
                    for tt in range(2):
                        act.wait_ge(conv_done, 2 * t + tt + 1)
                        if peeled == "loop" or t > 0:
                            act.wait_ge(hidden_done, 2 * t + tt - 1)
                        nc.scalar.activation(gelu[:, tt, :], conv[:, tt, :], ACT.Gelu_apprx_tanh).then_inc(gelu_done, 1)
                    if peeled == "last":
                        split_static(cu + RING, 1)
                    elif not first:
                        split_after(cu, slot_u)
                        split_after(cg, slot_g)
                    into = hT_hi[1 if peeled == "last" else 0]
                    for tt in range(2):
                        act.wait_ge(hidden_done, 2 * t + tt + 1)
                        if tt == 0 and peeled in ("second", "loop"):
                            act.wait_ge(chunk_used, cg + 2)
                        nc.scalar.activation(into[:, tt, :], hidden[:, tt, :], ACT.Copy).then_inc(hhi_done, 1)
                    if peeled == "last":
                        split_after(cg, slot_g)
                    if peeled in ("second", "loop"):
                        split_after(cg + 1, (slot_g + 1) % RING)

                ffn_group(0, "first")
                ffn_group(1, "second")
                with act.Fori(2, GROUPS - 1) as i:
                    ffn_group(i, "loop")
                ffn_group(GROUPS - 1, "last")
                if layer + 1 < LAYERS:
                    split_static(base + LAYER_CHUNKS + 1)
                    xT_hi_part(2 * layer + 2, (0, 1))
                    split_static(base + LAYER_CHUNKS + 2)
                    xT_hi_part(2 * layer + 2, (2, 3))
                else:
                    act.wait_ge(gained_done, 1)
                    act.wait_ge(std_done, ST * (2 * LAYERS - 1) + 1)
                    for half in range(2):
                        cols = slice(half * HALF, (half + 1) * HALF)
                        nc.scalar.activation(xs[:, 0, cols], xs[:, 0, cols], ACT.Copy,
                                             scale=std_inv[:, 0:1]).then_inc(scaled_done, 1)

        @block.vector
        def _(dve):
            steps = {"n": 0, "i": None, "per": 0}

            def link(ins):
                steps["n"] += 1
                ins.then_inc(dve_step, 1)
                if steps["i"] is None:
                    dve.wait_ge(dve_step, steps["n"])
                else:
                    dve.wait_ge(dve_step, steps["n"] + (steps["i"] - 2) * steps["per"])

            def split_lo(c, slot, part=slice(0, CHUNK), last=True):
                dve.wait_ge(hi_done, c + 1)
                count = 1
                if isinstance(c, int) and c - 1 in POOL_CHUNKS:
                    dve.wait_ge(pool_lo_done, pool_count(c - 1, 1))
                    count = 3 if c - 2 in POOL_CHUNKS else 2
                ins = nc.vector.tensor_tensor(w_lo[slot][:, part], raw[slot][:, part], w_hi[slot][:, part].bitcast(F32),
                                              ALU.subtract)
                if last:
                    ins.then_inc(lo_done, count)

            def split_static(c, half=None):
                part = slice(0, CHUNK) if half is None else slice(half * CHUNK // 2, (half + 1) * CHUNK // 2)
                if c < CHUNKS:
                    split_lo(c, c % RING, part, half != 0)

            def xT_lo_part(n, fills):
                for f in fills:
                    dve.wait_ge(xhi_done, 4 * n + f + 1)
                    st, half = divmod(f, 2)
                    part = (slice(None), slice(4 * half, 4 * half + 4), slice(st * P, (st + 1) * P))
                    nc.vector.tensor_tensor(xT_lo[part], side[f][:, :].rearrange("p (k q) -> p k q", k=4),
                                            xT_hi[part].bitcast(F32), ALU.subtract).then_inc(xlo_done, 1)

            def residual(n, st, half):
                part = xs[:, st, half * HALF:(half + 1) * HALF]
                if (st, half) == (1, 1):
                    dve.wait_ge(chunk_used, (n // 2) * LAYER_CHUNKS + (QKV_CHUNKS + WO_CHUNKS if n % 2 == 0
                                                                       else LAYER_CHUNKS))
                else:
                    dve.wait_ge(y_done, 3 * n + 2 * st + half + 1)
                link(nc.vector.scalar_tensor_tensor(part, part, ALPHA, wide[2 * st + half][:, :], ALU.mult, ALU.add))
                nc.vector.bn_stats(stats[:, st, half, :], part).then_inc(stats_done, 1)

            def layer_norm(n, st):
                dve.wait_ge(stats_done, 4 * n + 2 * st + 2)
                link(nc.vector.bn_aggr(moments[:, st, :], stats[:, st, :, :].rearrange("p a b -> p (a b)")))
                nc.vector.tensor_scalar(var_eps[:, st:st + 1], moments[:, st, 1:2], SUM_EPS, None,
                                        ALU.add).then_inc(var_done, 1)
                if st == 0:
                    dve.wait_ge(norm_in, 32 * (n // 2 + 1))
                for half in range(2):
                    cols = slice(half * HALF, (half + 1) * HALF)
                    last = nc.vector.scalar_tensor_tensor(xs[:, st, cols], xs[:, st, cols], moments[:, st, 0:1],
                                                          gain[:, n % 2, cols], ALU.subtract, ALU.mult)
                if (n, st) == (2 * LAYERS - 1, 0):
                    last.then_inc(gained_done, 1)
                    return
                link(last)
                dve.wait_ge(std_done, ST * n + st + 1)
                for half in range(2):
                    cols = slice(half * HALF, (half + 1) * HALF)
                    nc.vector.scalar_tensor_tensor(xs[:, st, cols], xs[:, st, cols], std_inv[:, st:st + 1],
                                                   shift[:, n % 2, cols], ALU.mult, ALU.add).then_inc(norm_x_done, 1)

            nc.vector.memset(zeros[:, :].bitcast(F32), 0.0).then_inc(zeros_done, 1)

            def first_piece(c, q):
                dve.wait_ge(*((hi_pieces, (PIECES - 1) * c + q + 1) if q < PIECES - 1 else (hi_done, c + 1)))
                part = slice(q * CHUNK // PIECES, (q + 1) * CHUNK // PIECES)
                nc.vector.tensor_tensor(w_lo[c][:, part], raw[c][:, part], w_hi[c][:, part].bitcast(F32),
                                        ALU.subtract).then_inc(lo_pieces if q < PIECES - 1 else lo_done, 1)

            for c in range(FIRST):
                for q in range(PIECES):
                    if c == 0 and q % 2 == 0:
                        xT_lo_part(0, (q // 2,))
                    elif c == 2 and q == 0:
                        xT_lo_part(0, (2, 3))
                    first_piece(c, q)

            dve.wait_ge(sines_done, 1)
            link(nc.vector.tensor_tensor(small[:, :, :], sines[:, 1], sines[:, 1], ALU.mult))
            for h in range(2):
                nc.vector.tensor_scalar(cos2[:, :, h * ROT:(h + 1) * ROT], small[:, :, :], -2.0, 1.0, ALU.mult, ALU.add)
                last = nc.vector.tensor_scalar(sin2[:, :, h * ROT:(h + 1) * ROT], sines[:, 0], 2.0 * h - 1.0, None,
                                               ALU.mult)
            link(last)
            dve.wait_ge(consts_done, 3)

            for layer in range(LAYERS):
                base = layer * LAYER_CHUNKS
                for kind, m, *rest in schedule[layer]["DVE"]:
                    if kind == "split_lo" and m == base + QKV_CHUNKS + WO_CHUNKS:
                        pass
                    elif kind == "split_lo":
                        split_static(m, rest[0])
                    elif kind == "rope":
                        dve.wait_ge(proj_drained, 12 * layer + 2 * m + 2)
                        for st in range(ST):
                            heads = rows[m % 3][:, st, :].rearrange("p (h d) -> p h d", d=64)

                            def over_heads(table, a, b):
                                return table[:, st, a:b].unsqueeze(1).broadcast_to([P, KT, b - a])

                            nc.vector.tensor_tensor(rot_a[:, st], heads[:, :, 0:2 * ROT],
                                                    over_heads(cos2, 0, 2 * ROT), ALU.mult)
                            nc.vector.tensor_tensor(rot_b[:, st, :, 0:ROT], heads[:, :, ROT:2 * ROT],
                                                    over_heads(sin2, 0, ROT), ALU.mult)
                            last = nc.vector.tensor_tensor(rot_b[:, st, :, ROT:2 * ROT], heads[:, :, 0:ROT],
                                                           over_heads(sin2, ROT, 2 * ROT), ALU.mult)
                        link(last)
                        for st in range(ST):
                            heads = rows[m % 3][:, st, :].rearrange("p (h d) -> p h d", d=64)
                            last = nc.vector.tensor_tensor(heads[:, :, 0:2 * ROT], rot_a[:, st], rot_b[:, st], ALU.add)
                        last.then_inc(rope_done, 1)
                    elif kind == "mask":
                        j = MAPS * layer + m
                        dve.wait_ge(scores_done, j + 1)
                        if j >= 2:
                            dve.wait_ge(exp_done, j - 1)
                        for q, (lo, hi) in enumerate(((0, P), (P, 3 * P))):
                            last = nc.vector.tensor_tensor_reduce(
                                out=masked[:, m % 2, lo:hi], in0=score_bank[m % 2][:, lo:hi], in1=causal[:, lo:hi],
                                scale=-SCALE, scalar=3e38, op0=ALU.add, op1=ALU.min,
                                accum_out=neg_max[:, m % 4, q:q + 1])
                        last.then_inc(max_done, 1)
                    elif kind == "norm" and layer == 0:
                        dve.wait_ge(exp_done, m + 1)
                        link(nc.vector.reciprocal(recips[:, m % 4, :], sums[:, m % 4, :]))
                        for q, (lo, hi) in enumerate(((0, P), (P, 3 * P))):
                            last = nc.vector.tensor_scalar(probs[:, m % 4, lo:hi], probs[:, m % 4, lo:hi],
                                                           recips[:, m % 4, q:q + 1], None, ALU.mult)
                        last.then_inc(norm_done, 1)
                    elif kind == "norm":
                        if m == 0:
                            dve.wait_ge(lam_exp_done, 1)
                            link(nc.vector.tensor_tensor(neg_lam[:, :], lam_exp[:, 1:2], lam_exp[:, 0:1], ALU.subtract))
                            link(nc.vector.tensor_scalar(neg_lam[:, :], neg_lam[:, :], LAMBDA_INIT, None, ALU.subtract))
                        a = 2 * (m % 2)
                        dve.wait_ge(exp_done, MAPS + 2 * m + 2)
                        link(nc.vector.reciprocal(recips[:, a, :], sums[:, a + 1, :]))
                        link(nc.vector.scalar_tensor_tensor(neg_lam_r[:, m % 2, :], sums[:, a, :], neg_lam[:, 0:1],
                                                            recips[:, a, :], ALU.mult, ALU.mult))
                        for q, (lo, hi) in enumerate(((0, P), (P, 3 * P))):
                            last = nc.vector.scalar_tensor_tensor(probs[:, a, lo:hi], probs[:, a + 1, lo:hi],
                                                                  neg_lam_r[:, m % 2, q:q + 1], probs[:, a, lo:hi],
                                                                  ALU.mult, ALU.add)
                        last.then_inc(norm_done, 1)
                        nc.vector.scalar_tensor_tensor(eps_sq[:, m % 4, :], sums[:, a, :], SUM_EPS, sums[:, a, :],
                                                       ALU.mult, ALU.mult).then_inc(eps_done, 1)
                    elif kind == "mean":
                        dve.wait_ge(squares_done, m + 1)
                        dve.wait_ge(eps_done, m + 1)
                        nc.vector.scalar_tensor_tensor(mean_sq[:, m % 2, :], mean_sq[:, m % 2, :], 1.0 / P,
                                                       eps_sq[:, m % 4, :], ALU.mult, ALU.add).then_inc(mean_sq_done, 1)
                    elif kind == "subln":
                        dve.wait_ge(rms_done, m + 1)
                        if m >= 1:
                            dve.wait_ge(turn_filled, fill_of[(1, "outT", m - 1)] + 1)
                        for st in range(ST):
                            last = nc.vector.tensor_scalar(head_out[:, st, :], head_rows[:, m % 2, st * P:(st + 1) * P],
                                                           rms_inv[:, m % 2, st:st + 1], None, ALU.mult)
                        last.then_inc(head_done, 1)
                    elif kind == "out_lo":
                        dve.wait_ge(ohi_done, 8 * layer + m + 1)
                        if layer == 0:
                            nc.vector.tensor_tensor(oT_lo[:, m, :], out_bank[:, 0:SEQ], oT_hi[:, m, :].bitcast(F32),
                                                    ALU.subtract).then_inc(olo_done, 1)
                        else:
                            nc.vector.scalar_tensor_tensor(oT_lo[:, m, :], turn_bank[:, 0:SEQ], sub_gain[:, 0:1],
                                                           oT_hi[:, m, :].bitcast(F32), ALU.mult,
                                                           ALU.subtract).then_inc(turn_drained, 1)
                n, c = 2 * layer, base + QKV_CHUNKS + WO_CHUNKS
                residual(n, 0, 0)
                residual(n, 0, 1)
                layer_norm(n, 0)
                residual(n, 1, 0)
                xT_lo_part(n + 1, (0, 1))
                residual(n, 1, 1)
                layer_norm(n, 1)
                xT_lo_part(n + 1, (2, 3))
                split_static(c + 2)

                def ffn_group(i, peeled):
                    t = GROUPS * layer + i
                    cu, cg = ffn_chunk(layer, i, 0), ffn_chunk(layer, i, 1)
                    at = 2 if peeled == "loop" else i
                    first = peeled == "first"
                    slot_u, slot_g = ffn_chunk(layer, at, 0) % RING, ffn_chunk(layer, at, 1) % RING

                    def split_after(c, slot):
                        if peeled == "loop":
                            split_lo(c + RING, slot)
                        else:
                            split_static(c + RING)

                    if first:
                        split_after(cu, slot_u)
                        split_after(cg, slot_g)
                    for tt in range(2):
                        up = up_of(first, tt)
                        dve.wait_ge(tap_done, 2 * t + tt + 1)
                        link(nc.vector.scalar_tensor_tensor(conv[:, tt, 1:SEQ], up[:, 0:SEQ - 1],
                                                            conv_cols[:, layer, bass.ds(FT + 2 * i + tt, 1)],
                                                            conv[:, tt, 1:SEQ], ALU.mult, ALU.add))
                        nc.vector.scalar_tensor_tensor(conv[:, tt, 2:SEQ], up[:, 0:SEQ - 2],
                                                       conv_cols[:, layer, bass.ds(2 * i + tt, 1)],
                                                       conv[:, tt, 2:SEQ], ALU.mult, ALU.add).then_inc(conv_done, 1)
                    b = 1 if peeled == "last" else 0

                    def make_hidden(tt):
                        dve.wait_ge(gelu_done, 2 * t + tt + 1)
                        if first:
                            dve.wait_ge(first_done, 2 * layer + tt + 1)
                        elif tt == 0:
                            dve.wait_ge(gate0_done, t - layer)
                        else:
                            dve.wait_ge(chunk_used, cg + 1)
                        if peeled == "loop" or t > 0:
                            dve.wait_ge(hhi_done, 2 * t + tt - 1)
                        nc.vector.tensor_tensor(hidden[:, tt, :], gelu[:, tt, :], gate_of(first, tt),
                                                ALU.mult).then_inc(hidden_done, 1)

                    def make_h_lo(tt):
                        dve.wait_ge(hhi_done, 2 * t + tt + 1)
                        nc.vector.tensor_tensor(hT_lo[b][:, tt, :], hidden[:, tt, :], hT_hi[b][:, tt, :].bitcast(F32),
                                                ALU.subtract).then_inc(hlo_done, 1)

                    if peeled == "last":
                        split_static(cu + RING)
                    elif not first:
                        split_after(cu, slot_u)
                    for tt in range(2):
                        make_hidden(tt)
                    if peeled in ("second", "loop"):
                        split_after(cg, slot_g)
                    for tt in range(2):
                        make_h_lo(tt)
                    if peeled in ("second", "loop"):
                        split_after(cg + 1, (slot_g + 1) % RING)

                ffn_group(0, "first")
                if layer == 0:
                    dve.wait_ge(small_in, 16 * 6)
                    link(nc.vector.tensor_tensor(lam_prod[:, :, :], lam_in[:, :, :].rearrange("p (a b) d -> p a b d", b=2)[:, :, 0, :],
                                                 lam_in[:, :, :].rearrange("p (a b) d -> p a b d", b=2)[:, :, 1, :], ALU.mult))
                    nc.vector.tensor_reduce(lam_dot[:, :], lam_prod[:, :, :], AX.X, ALU.add).then_inc(lam_dot_done, 1)
                    nc.vector.tensor_scalar(sub_gain[:, :], sub_g[:, :], 1.0 - LAMBDA_INIT, None, ALU.mult)
                ffn_group(1, "second")
                before = steps["n"]
                LINKS = 2
                with dve.Fori(2, GROUPS - 1) as i:
                    steps["i"], steps["per"] = i, LINKS
                    ffn_group(i, "loop")
                assert steps["n"] == before + LINKS
                steps["n"], steps["i"] = before + LINKS * (GROUPS - 3), None
                ffn_group(GROUPS - 1, "last")
                n, c = 2 * layer + 1, base + LAYER_CHUNKS
                residual(n, 0, 0)
                residual(n, 0, 1)
                layer_norm(n, 0)
                residual(n, 1, 0)
                if layer + 1 < LAYERS:
                    xT_lo_part(n + 1, (0, 1))
                split_static(c + 1)
                residual(n, 1, 1)
                layer_norm(n, 1)
                if layer + 1 < LAYERS:
                    xT_lo_part(n + 1, (2, 3))

        @block.tensor
        def _(pe):
            def product(dst, a_hi, a_lo, b_hi, b_lo, start, stop):
                nc.tensor.matmul(dst, a_hi, b_hi, start=start, stop=False, skip_group_check=True)
                nc.tensor.matmul(dst, a_hi, b_lo, start=False, stop=False, skip_group_check=True)
                return nc.tensor.matmul(dst, a_lo, b_hi, start=False, stop=stop, skip_group_check=True)

            def x_transposes(n, fills=range(4)):
                for f in fills:
                    st, half = divmod(f, 2)
                    if n == 0:
                        pe.wait_ge(x_in[st], 16)
                        pe.wait_ge(consts_done, 1)
                    else:
                        pe.wait_ge(norm_x_done, 4 * (n - 1) + f + 1)
                    for k in range(4):
                        last = nc.tensor.transpose(side[f][:, k * P:(k + 1) * P],
                                                   xs[:, st, (4 * half + k) * P:(4 * half + k + 1) * P], ident[:, :])
                    last.then_inc(xT_filled, 1)

            pe.wait_ge(zeros_done, 1)
            for products in WARM_UP:
                for n in range(products):
                    nc.tensor.matmul(wide[3][:, :], zeros[:, 0:P], zeros[:, :], start=True, stop=True)
                if products == WARM_UP[0]:
                    x_transposes(0, (0, 1))
            for layer in range(LAYERS):
                base = layer * LAYER_CHUNKS
                for kind, m, *rest in schedule[layer]["PE"]:
                    j = MAPS * layer + m
                    if kind == "proj":
                        cg, (kt, st) = m, rest
                        c = base + 2 * cg + kt // 4
                        if layer and (cg, kt, st) in ((0, 0, 0), (1, 2, 0)):
                            x_transposes(2 * layer, (1,) if cg == 0 else (2, 3))
                        if layer == 0 and (cg, kt, st) == (0, 6, 0):
                            x_transposes(0, (2, 3))
                        if cg == 0 and kt % 4 == 0:
                            pe.wait_ge(xlo_done, 8 * layer + 2 * st + kt // 4 + 1)
                        if c < FIRST and kt % 4 < PIECES - 1:
                            pe.wait_ge(lo_pieces, (PIECES - 1) * c + kt % 4 + 1)
                        elif c in POOL_CHUNKS:
                            if kt % 2 == 0:
                                pe.wait_ge(pool_lo_done, pool_count(c, kt // 2))
                        elif c < FIRST or kt % 4 == 0:
                            pe.wait_ge(lo_done, c + 1)
                        if kt == 0 and st == 0 and cg >= 2:
                            pe.wait_ge(proj_drained, 12 * layer + 2 * cg - 2)
                        cols = slice((kt % 4) * HALF, (kt % 4 + 1) * HALF)
                        rs = slice(st * P, (st + 1) * P)
                        last = product(wide[2 * (cg % 2) + st][:, :], xT_hi[:, kt, rs], xT_lo[:, kt, rs],
                                       w_hi[c % RING][:, cols], w_lo[c % RING][:, cols], kt == 0, kt == KT - 1)
                        if kt % 4 == 3 and st == 1:
                            last.then_inc(chunk_used, 1)
                    elif kind == "qkT":
                        cg, f = m, rest[0]
                        n = fill_of[(layer, "qkT", cg, f)]
                        g, mat = divmod(cg, 3)
                        if f == 0:
                            pe.wait_ge(rope_done, 4 * layer + 2 * g + mat + 1)
                        if n:
                            pe.wait_ge(turn_drained, n)
                        for k in range(2):
                            for st in range(ST):
                                last = nc.tensor.transpose(turn_bank[:, (2 * k + st) * P:(2 * k + st + 1) * P],
                                                           rows[mat][:, st, (2 * f + k) * P:(2 * f + k + 1) * P],
                                                           ident[:, :])
                        last.then_inc(turn_filled, 1)
                    elif kind == "scores":
                        half = slice(64 * (m % 2), 64 * (m % 2) + 64)
                        qT, kT = headT[0][half, m // 2, :], headT[1][half, m // 2, :]
                        if m % 4 == 0:
                            g, f = m // 8, m // 4 % 2
                            for cg in (3 * g, 3 * g + 1):
                                pe.wait_ge(turn_drained, fill_of[(layer, "qkT", cg, f)] + 1)
                        if layer == 0 and m == 0:
                            pe.wait_ge(small_in, 16 * 6)
                            for n in range(LAYERS):
                                last = nc.tensor.transpose(out_bank[:, 4 * FT * n:4 * FT * (n + 1)], conv_rows[:, n, :],
                                                           ident[0:4 * FT, 0:4 * FT])
                            last.then_inc(cols_filled, 1)
                        if j >= 2:
                            pe.wait_ge(max_done, j - 1)
                        bank_ = score_bank[m % 2]
                        nc.tensor.matmul(bank_[:, 0:P], qT[:, 0:P], kT[:, 0:P], start=True, stop=True)
                        nc.tensor.matmul(bank_[:, P:3 * P], qT[:, P:2 * P], kT[:, :], start=True,
                                         stop=True).then_inc(scores_done, 1)
                    elif kind == "probT":
                        n = fill_of[(layer, "probT", m)]
                        slot = m % 4 if layer == 0 else 2 * (m % 2)
                        pe.wait_ge(norm_done, (0 if layer == 0 else MAPS) + m + 1)
                        pe.wait_ge(turn_drained, n)
                        for b in range(3):
                            last = nc.tensor.transpose(turn_bank[:, b * P:(b + 1) * P], probs[:, slot, b * P:(b + 1) * P],
                                                       ident[:, :])
                        last.then_inc(turn_filled, 1)
                    elif kind == "pv":
                        pe.wait_ge(turn_drained, fill_of[(layer, "probT", m)] + 1)
                        if layer == 0 and m % 8 == 0 or layer == 1 and m % 4 == 0:
                            g = m // 8 if layer == 0 else m // 4
                            pe.wait_ge(proj_drained, 12 * layer + 6 * g + 6)
                        pT = probsT[:, m % 2, :]
                        if layer == 0:
                            if m == 0:
                                pe.wait_ge(cols_drained, 1)
                            if m % 2 == 0 and m >= 2:
                                pe.wait_ge(olo_done, m // 2)
                            part = out_bank[64 * (m % 2):64 * (m % 2) + 64, :]
                            nc.tensor.matmul(part[:, 0:SEQ], v_rows[:, 0, 64 * m:64 * m + 64], pT[:, 0:SEQ], start=True,
                                             stop=False)
                            nc.tensor.matmul(part[:, P:SEQ], v_rows[:, 1, 64 * m:64 * m + 64], pT[:, SEQ:3 * P],
                                             start=False, stop=True).then_inc(pv_done, 1)
                        else:
                            if m == 0:
                                pe.wait_ge(olo_done, 8)
                            else:
                                pe.wait_ge(head_rows_done, m)
                            v = [v_rows[:, st, P * m:P * (m + 1)] for st in range(ST)]
                            nc.tensor.matmul(out_bank[:, 0:P], pT[:, 0:P], v[0], start=True, stop=True)
                            nc.tensor.matmul(out_bank[:, P:SEQ], pT[:, P:SEQ], v[0], start=True, stop=False)
                            nc.tensor.matmul(out_bank[:, P:SEQ], pT[:, SEQ:3 * P], v[1], start=False,
                                             stop=True).then_inc(pv_done, 1)
                    elif kind == "outT":
                        pe.wait_ge(head_done, m + 1)
                        pe.wait_ge(turn_drained, fill_of[(1, "outT", m)])
                        for st in range(ST):
                            last = nc.tensor.transpose(turn_bank[:, st * P:(st + 1) * P], head_out[:, st, :], ident[:, :])
                        last.then_inc(turn_filled, 1)
                    elif kind == "wo":
                        kt, (st, half) = m, rest
                        c = base + QKV_CHUNKS + kt // 2
                        if (kt, st, half) == (6, 1, 1):
                            x_transposes(2 * layer + 1, (0, 1))
                        if st == 0 and half == 0:
                            if layer == 0:
                                pe.wait_ge(olo_done, kt + 1)
                            else:
                                pe.wait_ge(turn_drained, fill_of[(1, "outT", kt)] + 1)
                            if kt % 2 == 0:
                                pe.wait_ge(lo_done, c + 1)
                        if kt == 0 and half == 0:
                            pe.wait_ge(proj_drained, 12 * layer + 10 + 2 * st)
                        rs = slice(st * P, (st + 1) * P)
                        cols = slice((2 * (kt % 2) + half) * HALF, (2 * (kt % 2) + half + 1) * HALF)
                        last = product(wide[2 * st + half][:, :], oT_hi[:, kt, rs], oT_lo[:, kt, rs],
                                       w_hi[c % RING][:, cols], w_lo[c % RING][:, cols], kt == 0, kt == KT - 1)
                        if st == 1 and half == 1 and kt % 2 == 1:
                            last.then_inc(chunk_used, 1)
                        elif kt == KT - 1:
                            last.then_inc(y_done, 1)

                cu, cg = ffn_chunk(layer, 0, 0), ffn_chunk(layer, 0, 1)
                for st in range(ST):
                    for n, c in enumerate((cu, cg)):
                        for kt in range(KT):
                            if st == 0 and kt % 4 == 0:
                                pe.wait_ge(pool_lo_done, pool_count(c, kt // 4))
                            if (st, n, kt) == (0, 1, 6):
                                x_transposes(2 * layer + 1, (2, 3))
                            if n == 0 and kt % 4 == 0:
                                pe.wait_ge(xlo_done, 8 * layer + 4 + 2 * st + kt // 4 + 1)
                            rs = slice(st * P, (st + 1) * P)
                            cols = slice(kt * 2 * P, (kt + 1) * 2 * P)
                            last = product(wide[st][:, n * 2 * P:(n + 1) * 2 * P], xT_hi[:, kt, rs], xT_lo[:, kt, rs],
                                           w_hi[c % RING][:, cols], w_lo[c % RING][:, cols], kt == 0, kt == KT - 1)
                        if st == 1:
                            last.then_inc(chunk_used, 1)
                        elif n == 1:
                            last.then_inc(tokens_done, 1)

                def features(banks, slot, free, done0, between=None):
                    for tt in range(2):
                        if free is not None:
                            pe.wait_ge(*free[tt])
                        for kt in range(KT):
                            cols = slice(kt * 2 * P + tt * P, kt * 2 * P + (tt + 1) * P)
                            last = product(banks[tt][:, 0:SEQ], w_hi[slot][:, cols], w_lo[slot][:, cols],
                                           xT_hi[:, kt, :], xT_lo[:, kt, :], kt == 0, kt == KT - 1)
                        last.then_inc(done0 if tt == 0 else chunk_used, 1)
                        if tt == 0 and between:
                            between()

                def first_group_transposes():
                    pe.wait_ge(tokens_out, ST * (layer + 1))
                    for tt in range(2):
                        for which in range(2):
                            for st in range(ST):
                                col = (2 * which + tt) * P
                                last = nc.tensor.transpose(wide[2 + tt][:, which * SEQ + st * P:which * SEQ + (st + 1) * P],
                                                           token_rows[:, st, col:col + P], ident[:, :])
                        last.then_inc(first_done, 1)

                def zero_y():
                    pe.wait_ge(conv_done, 2 * GROUPS * layer + 2)
                    pe.wait_ge(hidden_done, 2 * GROUPS * layer + 2)
                    for b in range(4):
                        nc.tensor.matmul(wide[b][:, :], zeros[:, 0:P], zeros[:, :], start=True, stop=True)

                def second_product(slot, b, st, half, stop=False):
                    rs = slice(st * P, (st + 1) * P)
                    for tt in range(2):
                        cols = slice((2 * tt + half) * HALF, (2 * tt + half + 1) * HALF)
                        last = product(wide[2 * st + half][:, :], hT_hi[b][:, tt, rs], hT_lo[b][:, tt, rs],
                                       w_hi[slot][:, cols], w_lo[slot][:, cols], False, stop and tt == 1)
                    return last

                def second_ready(i):
                    pe.wait_ge(lo_done, ffn_chunk(layer, i, 2) + 1)
                    pe.wait_ge(hlo_done, 2 * (GROUPS * layer + i) + 2)

                def ffn_group(i, peeled):
                    t = GROUPS * layer + i
                    at = 2 if peeled == "loop" else i
                    second = peeled == "second"
                    slot_g = ffn_chunk(layer, at, 1) % RING
                    pe.wait_ge(lo_done, ffn_chunk(layer, i, 0) + 1)
                    features(up_bank, ffn_chunk(layer, at, 0) % RING,
                             None if second else [(conv_done, 2 * t - 1), (conv_done, 2 * t)], up0_done,
                             first_group_transposes if second else None)
                    pe.wait_ge(lo_done, ffn_chunk(layer, i, 1) + 1)
                    features(gate_bank, slot_g,
                             None if second else [(hidden_done, 2 * t - 1), (hidden_done, 2 * t)], gate0_done)
                    if second:
                        zero_y()
                    if peeled != "last":
                        second_ready(i - 1)
                        for st in range(ST):
                            for half in range(2):
                                last = second_product((slot_g + 1) % RING, 0, st, half)
                        last.then_inc(chunk_used, 1)

                ffn_group(1, "second")
                with pe.Fori(2, GROUPS - 1) as i:
                    ffn_group(i, "loop")
                ffn_group(GROUPS - 1, "last")
                for i, st, half in ([(GROUPS - 2, 0, 0), (GROUPS - 2, 0, 1), (GROUPS - 1, 0, 0), (GROUPS - 1, 0, 1)]
                                    + [(i, 1, half) for half in range(2) for i in (GROUPS - 2, GROUPS - 1)]):
                    if (st, half) == (0, 0):
                        second_ready(i)
                    final = i == GROUPS - 1
                    if layer + 1 < LAYERS and (i, st, half) == (GROUPS - 1, 1, 1):
                        x_transposes(2 * layer + 2, (0,))
                    last = second_product(ffn_chunk(layer, i, 2) % RING, int(final), st, half, final)
                    if (st, half) == (1, 1):
                        last.then_inc(chunk_used, 1)
                    elif final:
                        last.then_inc(y_done, 1)


_INS = ["x", "positions", "a_w_qkv", "a_w_o", "w_kv_shared", "b_w_q", "b_w_o", "b_lambda", "b_subln_g", "ln_g",
        "ln_b", "ffn_w_in", "ffn_conv_w", "ffn_conv_b", "ffn_w_out"]


def kernel(**inputs):
    from concourse import bacc
    from concourse.bass_utils import run_bass_kernel_spmd

    nc = bacc.Bacc("TRN2", target_bir_lowering=False, num_devices=1)
    arrays, args = {}, []
    for name in _INS:
        a = np.ascontiguousarray(inputs[name])
        arrays[f"in_{name}"] = a
        args.append(nc.dram_tensor(f"in_{name}", a.shape, mybir.dt.from_np(a.dtype), kind="ExternalInput").ap())
    shape = inputs["x"].shape
    args.append(nc.dram_tensor("out_0", shape, F32, kind="ExternalOutput").ap())
    yoco_trunk(nc, *args)
    r = run_bass_kernel_spmd(nc, [arrays], core_ids=[0])
    return r.results[0]["out_0"]
```
